# Optimizing a Trainium2 kernel written in Bass

```python
import jax, jax.numpy as jnp
from jax import lax
import numpy as np

D_MODEL = 2048
BATCH = 1
SEQ = 256
DEPTH = 1

CHUNK = 64
Q_BLOCK = 128
N_MIXERS = 3
RMS_EPS = 1e-6
SB_HEADS = 16
SB_HEAD_DIM = D_MODEL // SB_HEADS
HG_HEADS = 16
HG_KEY_DIM = D_MODEL // HG_HEADS
HG_VAL_DIM = D_MODEL // HG_HEADS
HG_WIDTH = HG_HEADS * HG_KEY_DIM
MLA_HEADS = 16
MLA_NOPE = 128
MLA_ROPE = 64
MLA_V = 128
MLA_Q_RANK = 768
MLA_KV_RANK = 512
ROPE_THETA = 10000.0
D_FF = 4 * D_MODEL


def _n_layers_of(m):
    return len(range(m, DEPTH, N_MIXERS))

def rms_norm(x, g):
    xf = x.astype(jnp.float32)
    y = xf * lax.rsqrt(jnp.mean(xf * xf, axis=-1, keepdims=True) + RMS_EPS)
    return (y * g.astype(jnp.float32)).astype(x.dtype)

def _sweep_query_blocks(block_fn, queries):
    B, S = queries[0].shape[:2]
    nb = S // Q_BLOCK
    blocked = tuple(a.reshape(B, nb, Q_BLOCK, *a.shape[2:]).swapaxes(0, 1) for a in queries)
    starts = jnp.arange(nb, dtype=jnp.int32) * Q_BLOCK
    out = lax.map(lambda xs: block_fn(xs[0], *xs[1]), (starts, blocked))
    return out.swapaxes(0, 1).reshape(B, S, *out.shape[3:])

def stick_breaking_mixer(h, w_qkv, w_o):
    B, S, _ = h.shape
    qkv = h @ w_qkv
    q, k, v = [a.reshape(B, S, SB_HEADS, SB_HEAD_DIM) for a in jnp.split(qkv, 3, axis=-1)]
    key_idx = jnp.arange(S)
    scale = SB_HEAD_DIM ** -0.5

    def block(q0, qb):
        z = jnp.einsum('bqhd,bkhd->bhqk', qb, k).astype(jnp.float32) * scale
        t = q0 + jnp.arange(Q_BLOCK)
        mask = key_idx[None, :] < t[:, None]
        log_one_minus = jnp.where(mask, -jax.nn.softplus(z), 0.0)
        after = lax.cumsum(log_one_minus, axis=3, reverse=True) - log_one_minus
        A = jnp.where(mask, jnp.exp(jax.nn.log_sigmoid(z) + after), 0.0)
        return jnp.einsum('bhqk,bkhd->bqhd', A.astype(v.dtype), v)

    o = _sweep_query_blocks(block, (q,))
    return o.reshape(B, S, SB_HEADS * SB_HEAD_DIM) @ w_o

def hgrn2_mixer(h, w_in, g_norm, w_o, lb):
    B, S, _ = h.shape
    N = S // CHUNK
    proj = h @ w_in
    q, fz, i, g = jnp.split(proj, [HG_WIDTH, 2 * HG_WIDTH, 2 * HG_WIDTH + HG_HEADS * HG_VAL_DIM], axis=-1)
    fz = fz.astype(jnp.float32)
    log_f = jnp.logaddexp(jnp.log(lb), jnp.log1p(-lb) + jax.nn.log_sigmoid(fz))
    k = (1.0 - lb) * jax.nn.sigmoid(-fz)

    def to_chunks(a, d):
        return a.astype(jnp.float32).reshape(B, N, CHUNK, HG_HEADS, d).transpose(1, 0, 3, 2, 4)

    xs = (to_chunks(q, HG_KEY_DIM), to_chunks(k, HG_KEY_DIM),
          to_chunks(i, HG_VAL_DIM), to_chunks(log_f, HG_KEY_DIM))
    causal = jnp.tril(jnp.ones((CHUNK, CHUNK), dtype=bool))[None, None, :, :, None]

    def step(state, chunk):
        qc, kc, vc, lfc = chunk
        b = jnp.cumsum(lfc, axis=2)
        b_last = b[:, :, -1:, :]
        o_inter = jnp.einsum('bhtc,bhcv->bhtv', qc * jnp.exp(b), state)
        diff = jnp.where(causal, b[:, :, :, None, :] - b[:, :, None, :, :], -jnp.inf)
        scores = jnp.einsum('bhtc,bhsc,bhtsc->bhts', qc, kc, jnp.exp(diff))
        o_intra = jnp.einsum('bhts,bhsv->bhtv', scores, vc)
        new_state = (jnp.exp(b_last[:, :, 0, :])[..., None] * state
                     + jnp.einsum('bhsc,bhsv->bhcv', kc * jnp.exp(b_last - b), vc))
        return new_state, o_inter + o_intra

    state0 = jnp.zeros((B, HG_HEADS, HG_KEY_DIM, HG_VAL_DIM), jnp.float32)
    _, o = lax.scan(step, state0, xs)
    o = o.transpose(1, 0, 3, 2, 4).reshape(B, S, HG_HEADS, HG_VAL_DIM)
    o = o * lax.rsqrt(jnp.mean(o * o, axis=-1, keepdims=True) + RMS_EPS) * g_norm.astype(jnp.float32)
    o = o.reshape(B, S, HG_HEADS * HG_VAL_DIM) * jax.nn.silu(g.astype(jnp.float32))
    return o.astype(h.dtype) @ w_o

def _rope_cos_sin(positions):
    inv_freq = ROPE_THETA ** (-jnp.arange(0, MLA_ROPE, 2, dtype=jnp.float32) / MLA_ROPE)
    ang = positions.astype(jnp.float32)[..., None] * inv_freq
    return jnp.cos(ang), jnp.sin(ang)

def _apply_rope(x, cos, sin):
    x1, x2 = jnp.split(x.astype(jnp.float32), 2, axis=-1)
    return jnp.concatenate([x1 * cos - x2 * sin, x1 * sin + x2 * cos], axis=-1).astype(x.dtype)

def mla_mixer(h, positions, w_dkv, q_norm, kv_norm, w_uq, w_ukv, w_o):
    B, S, _ = h.shape
    c_q, c_kv, k_pe = jnp.split(h @ w_dkv, [MLA_Q_RANK, MLA_Q_RANK + MLA_KV_RANK], axis=-1)
    c_q = rms_norm(c_q, q_norm)
    c_kv = rms_norm(c_kv, kv_norm)
    q = (c_q @ w_uq).reshape(B, S, MLA_HEADS, MLA_NOPE + MLA_ROPE)
    q_nope, q_pe = q[..., :MLA_NOPE], q[..., MLA_NOPE:]
    kv = (c_kv @ w_ukv).reshape(B, S, MLA_HEADS, MLA_NOPE + MLA_V)
    k_nope, v = kv[..., :MLA_NOPE], kv[..., MLA_NOPE:]
    cos, sin = _rope_cos_sin(positions)
    q_pe = _apply_rope(q_pe, cos[:, :, None, :], sin[:, :, None, :])
    k_pe = _apply_rope(k_pe, cos, sin)
    key_chunk = jnp.arange(S) // CHUNK
    scale = (MLA_NOPE + MLA_ROPE) ** -0.5

    def block(q0, qn, qp):
        s = (jnp.einsum('bqhd,bkhd->bhqk', qn, k_nope)
             + jnp.einsum('bqhr,bkr->bhqk', qp, k_pe)).astype(jnp.float32) * scale
        q_chunk = (q0 + jnp.arange(Q_BLOCK)) // CHUNK
        mask = key_chunk[None, :] <= q_chunk[:, None]
        p = jax.nn.softmax(jnp.where(mask, s, -jnp.inf), axis=-1)
        return jnp.einsum('bhqk,bkhd->bqhd', p.astype(v.dtype), v)

    o = _sweep_query_blocks(block, (q_nope, q_pe))
    return o.reshape(B, S, MLA_HEADS * MLA_V) @ w_o

def sq_relu_mlp(h, w1, w2):
    return jnp.square(jax.nn.relu(h @ w1)) @ w2

def first_inputs(seed: int = 0) -> dict:
    key = jax.random.key(seed)
    ks = jax.random.split(key, 20)
    n_sb, n_hg, n_mla = _n_layers_of(0), _n_layers_of(1), _n_layers_of(2)

    def w(k, shape, fan_in):
        return jax.random.normal(k, shape, jnp.float32) * (fan_in ** -0.5)

    def gain(k, shape):
        return 1.0 + 0.02 * jax.random.normal(k, shape, jnp.float32)

    return {
        "x": jax.random.normal(ks[0], (BATCH, SEQ, D_MODEL), jnp.float32),
        "positions": jnp.broadcast_to(jnp.arange(SEQ, dtype=jnp.int32), (BATCH, SEQ)),
        "norm_mix": gain(ks[1], (DEPTH, D_MODEL)),
        "norm_mlp": gain(ks[2], (DEPTH, D_MODEL)),
        "final_norm": gain(ks[3], (D_MODEL,)),
        "sb_w_qkv": w(ks[4], (n_sb, D_MODEL, 3 * SB_HEADS * SB_HEAD_DIM), D_MODEL),
        "sb_w_o": w(ks[5], (n_sb, SB_HEADS * SB_HEAD_DIM, D_MODEL), SB_HEADS * SB_HEAD_DIM),
        "hg_w_in": w(ks[6], (n_hg, D_MODEL, 3 * HG_WIDTH + HG_HEADS * HG_VAL_DIM), D_MODEL),
        "hg_lb_logits": 0.5 * jax.random.normal(ks[7], (DEPTH, HG_WIDTH), jnp.float32),
        "hg_g_norm": gain(ks[8], (n_hg, HG_VAL_DIM)),
        "hg_w_o": w(ks[9], (n_hg, HG_HEADS * HG_VAL_DIM, D_MODEL), HG_HEADS * HG_VAL_DIM),
        "mla_w_dkv": w(ks[10], (n_mla, D_MODEL, MLA_Q_RANK + MLA_KV_RANK + MLA_ROPE), D_MODEL),
        "mla_q_norm": gain(ks[11], (n_mla, MLA_Q_RANK)),
        "mla_kv_norm": gain(ks[12], (n_mla, MLA_KV_RANK)),
        "mla_w_uq": w(ks[13], (n_mla, MLA_Q_RANK, MLA_HEADS * (MLA_NOPE + MLA_ROPE)), MLA_Q_RANK),
        "mla_w_ukv": w(ks[14], (n_mla, MLA_KV_RANK, MLA_HEADS * (MLA_NOPE + MLA_V)), MLA_KV_RANK),
        "mla_w_o": w(ks[15], (n_mla, MLA_HEADS * MLA_V, D_MODEL), MLA_HEADS * MLA_V),
        "mlp_w1": w(ks[16], (DEPTH, D_MODEL, D_FF), D_MODEL),
        "mlp_w2": w(ks[17], (DEPTH, D_FF, D_MODEL), D_FF),
    }

def first_block(x, positions, norm_mix, norm_mlp, final_norm, sb_w_qkv, sb_w_o, hg_w_in,
              hg_lb_logits, hg_g_norm, hg_w_o, mla_w_dkv, mla_q_norm, mla_kv_norm,
              mla_w_uq, mla_w_ukv, mla_w_o, mlp_w1, mlp_w2):
    p_lb = jax.nn.softmax(hg_lb_logits.astype(jnp.float32), axis=0)
    lb_all = jnp.cumsum(p_lb, axis=0) - p_lb[0]
    h = x
    for i in range(DEPTH):
        m, j = i % N_MIXERS, i // N_MIXERS
        a = rms_norm(h, norm_mix[i])
        if m == 0:
            y = stick_breaking_mixer(a, sb_w_qkv[j], sb_w_o[j])
        elif m == 1:
            y = hgrn2_mixer(a, hg_w_in[j], hg_g_norm[j], hg_w_o[j], lb_all[i])
        else:
            y = mla_mixer(a, positions, mla_w_dkv[j], mla_q_norm[j], mla_kv_norm[j],
                          mla_w_uq[j], mla_w_ukv[j], mla_w_o[j])
        h = h + y
        h = h + sq_relu_mlp(rms_norm(h, norm_mlp[i]), mlp_w1[i], mlp_w2[i])
    return rms_norm(h, final_norm)


N_META = 16
POOL_WIDTH = D_MODEL
POOL_WINDOWS = (2, 4, 8, 16)
N_POOL_GROUPS = len(POOL_WINDOWS)
POOL_GROUP = POOL_WIDTH // N_POOL_GROUPS
CONV_WIDTH = D_MODEL
CONV_K = 3
N_BRANCHES = 2
FFN_HIDDEN = ((8 * D_MODEL // 3 + 255) // 256) * 256
IN_PROJ_WIDTH = POOL_WIDTH + 3 * CONV_WIDTH + N_BRANCHES * D_MODEL
EPS = 1e-6


def rms_norm_2(x, g):
    xf = x.astype(jnp.float32)
    y = xf * lax.rsqrt(jnp.mean(xf * xf, axis=-1, keepdims=True) + EPS)
    return (y * g.astype(jnp.float32)).astype(x.dtype)

def causal_multiscale_pool(u):
    b, l, _ = u.shape
    ug = u.reshape(b, l, N_POOL_GROUPS, POOL_GROUP).astype(jnp.float32)
    c = jnp.concatenate([jnp.zeros((b, 1, N_POOL_GROUPS, POOL_GROUP), jnp.float32),
                         jnp.cumsum(ug, axis=1)], axis=1)
    t1 = jnp.arange(1, l + 1, dtype=jnp.float32)
    outs = []
    for gi, w in enumerate(POOL_WINDOWS):
        cg = c[:, :, gi]
        c_lag = jnp.pad(cg, ((0, 0), (w - 1, 0), (0, 0)))[:, :l]
        win_sum = cg[:, 1:] - c_lag
        count = jnp.minimum(t1, jnp.float32(w))[None, :, None]
        outs.append(win_sum / count - ug[:, :, gi])
    return jnp.stack(outs, axis=2).astype(u.dtype)

def causal_depthwise_conv(v, w):
    l = v.shape[1]
    vp = jnp.pad(v, ((0, 0), (CONV_K - 1, 0), (0, 0)))
    return sum(w[k][None, None, :] * vp[:, k:k + l] for k in range(CONV_K))

def second_inputs(seed: int = 0) -> dict:
    key = jax.random.key(seed)
    ks = jax.random.split(key, 16)
    f32 = jnp.float32
    nrm = lambda k, shape, scale: jax.random.normal(k, shape, f32) * scale
    return {
        "x": nrm(ks[0], (BATCH, SEQ, D_MODEL), 1.0),
        "meta_tokens": nrm(ks[1], (N_META, D_MODEL), 1.0),
        "norm_mix_g": 1.0 + nrm(ks[2], (D_MODEL,), 0.02),
        "w_in": nrm(ks[3], (D_MODEL, IN_PROJ_WIDTH), D_MODEL ** -0.5),
        "b_gate": nrm(ks[4], (N_BRANCHES * D_MODEL,), 0.02),
        "pool_w": nrm(ks[5], (N_POOL_GROUPS, POOL_GROUP, POOL_GROUP), POOL_GROUP ** -0.5),
        "pool_scale": 1.0 + nrm(ks[6], (POOL_WIDTH,), 0.02),
        "conv_w": nrm(ks[7], (CONV_K, CONV_WIDTH), CONV_K ** -0.5),
        "conv_out_w": nrm(ks[8], (CONV_WIDTH, D_MODEL), CONV_WIDTH ** -0.5),
        "w_o": nrm(ks[9], (D_MODEL, D_MODEL), D_MODEL ** -0.5),
        "norm_ffn_g": 1.0 + nrm(ks[10], (D_MODEL,), 0.02),
        "w_gate_up": nrm(ks[11], (D_MODEL, 2 * FFN_HIDDEN), D_MODEL ** -0.5),
        "w_down": nrm(ks[12], (FFN_HIDDEN, D_MODEL), FFN_HIDDEN ** -0.5),
        "norm_final_g": 1.0 + nrm(ks[13], (D_MODEL,), 0.02),
    }

def second_block(x, meta_tokens, norm_mix_g, w_in, b_gate, pool_w, pool_scale, conv_w,
              conv_out_w, w_o, norm_ffn_g, w_gate_up, w_down, norm_final_g):
    b = x.shape[0]
    meta = jnp.broadcast_to(meta_tokens[None].astype(x.dtype), (b, N_META, D_MODEL))
    h = jnp.concatenate([meta, x], axis=1)

    splits = np.cumsum([POOL_WIDTH, CONV_WIDTH, CONV_WIDTH, CONV_WIDTH, D_MODEL]).tolist()
    for _ in range(DEPTH):
        hn = rms_norm_2(h, norm_mix_g)
        proj = hn @ w_in
        u, gb_in, gc_in, v_in, ga_lin, gbr_lin = jnp.split(proj, splits, axis=-1)

        pooled = causal_multiscale_pool(u)
        y_a = jnp.einsum("blgc,gcd->blgd", pooled, pool_w).reshape(b, -1, POOL_WIDTH)
        y_a = y_a * pool_scale

        y_b = (gb_in * causal_depthwise_conv(gc_in * v_in, conv_w)) @ conv_out_w

        gates = jax.nn.sigmoid(jnp.concatenate([ga_lin, gbr_lin], axis=-1) + b_gate)
        g_a, g_b = jnp.split(gates, 2, axis=-1)
        h = h + (g_a * y_a + g_b * y_b) @ w_o

        hn = rms_norm_2(h, norm_ffn_g)
        gate, up = jnp.split(hn @ w_gate_up, 2, axis=-1)
        h = h + (jax.nn.silu(gate) * up) @ w_down

    out = rms_norm_2(h, norm_final_g)
    return out[:, N_META:]


def setup_inputs(seed=0):
    out = dict(first_inputs(seed))
    for name, value in second_inputs(seed + 1).items():
        if name != "x":
            out[name + "_2"] = value
    return out


def reference(
    x, positions, norm_mix, norm_mlp, final_norm, sb_w_qkv, sb_w_o, hg_w_in, hg_lb_logits,
    hg_g_norm, hg_w_o, mla_w_dkv, mla_q_norm, mla_kv_norm, mla_w_uq, mla_w_ukv, mla_w_o, mlp_w1,
    mlp_w2, meta_tokens_2, norm_mix_g_2, w_in_2, b_gate_2, pool_w_2, pool_scale_2, conv_w_2,
    conv_out_w_2, w_o_2, norm_ffn_g_2, w_gate_up_2, w_down_2, norm_final_g_2,
):
    x = first_block(
        x, positions, norm_mix, norm_mlp, final_norm, sb_w_qkv, sb_w_o, hg_w_in, hg_lb_logits,
        hg_g_norm, hg_w_o, mla_w_dkv, mla_q_norm, mla_kv_norm, mla_w_uq, mla_w_ukv, mla_w_o,
        mlp_w1, mlp_w2,
    )
    return second_block(
        x, meta_tokens_2, norm_mix_g_2, w_in_2, b_gate_2, pool_w_2, pool_scale_2, conv_w_2,
        conv_out_w_2, w_o_2, norm_ffn_g_2, w_gate_up_2, w_down_2, norm_final_g_2,
    )


_drawn_inputs = setup_inputs


def setup_inputs(seed=0):
    import zlib

    import numpy as np

    out = dict(_drawn_inputs(seed))
    spreads = {}
    factors = {'norm_mix': 2.962,
     'norm_mix_g_2': 2.971,
     'b_gate_2': 8.0,
     'pool_scale_2': 31.704,
     'norm_ffn_g_2': 15.14,
     'norm_final_g_2': 7.751,
     'norm_mlp': 3.129}
    for name, (base, spread) in spreads.items():
        noise = np.random.default_rng([zlib.crc32(name.encode()), seed]).standard_normal(out[name].shape)
        drawn = base * np.exp(spread * noise) if base else spread * noise
        out[name] = __import__('jax').numpy.asarray(drawn.astype(out[name].dtype))
    for name, factor in factors.items():
        out[name] = (out[name] * factor).astype(out[name].dtype)
    return out
```

```python
from contextlib import ExitStack

import concourse.bass as bass
from concourse import mybir

ALU = mybir.AluOpType
ACT = mybir.ActivationFunctionType
F32 = mybir.dt.float32
F32R = mybir.dt.float32r

P = 128
D = 2048
NT = D // P
T = 256
MT = T // P
M = 16
TW = M + T
HD = 128
HEADS = D // HD
GH = 4
KT = 4
PW = 512
JT = PW // P
CH = D // (KT * P)
D_FF = 4 * D
FFN = 5632
WINDOWS = (2, 4, 8, 16)
EPS = 1e-6
QK_SCALE = HD ** -0.5
RAW = 4
SPLIT = 2
AHEAD = 2

KINDS = {
    "x": dict(full=1, act=1, pool=1, mid=1),
    "q": dict(full=1, act=1, pool=1),
    "k": dict(full=1, act=1, pool=1),
    "v": dict(full=1, act=1, pool=1),
    "attn": dict(full=1, act=1, pool=1, mid=1),
    "res": dict(full=1, act=1, pool=1, mid=1, sq=2),
    "resb": dict(full=1, act=1, pool=1, mid=1, sq=2),
    "res2": dict(full=1, act=1, pool=1, mid=2, sq=4),
    "add": dict(full=1),
    "relu2": dict(full=1, act=1, pool=1, mid=1),
    "u0": dict(full=1, act=1, pool=1, mid=2),
    "u1": dict(full=1, act=1, pool=1, mid=3),
    "u2": dict(full=1, act=1, pool=1, mid=4),
    "u3": dict(full=1, act=1, pool=1, mid=5),
    "ga": dict(full=1, act=1, mid=2),
    "pw": dict(full=1, mid=1),
    "gc": dict(full=1),
    "vv": dict(full=1, act=1, mid=4),
    "gb": dict(full=1, act=1, pool=1, mid=1),
    "gbr": dict(full=1, act=1, mid=1),
    "co": dict(full=1, act=1, pool=1, mid=1),
    "gate": dict(full=1, act=1, pool=1),
    "up": dict(full=1, act=1, pool=1, mid=1),
    "fin": dict(full=1, act=1, mid=1, sq=2),
}
WIDE = ("u0", "u1", "u2", "u3", "gc", "vv")
NORM_AT = (2, 3, 5, 6)
NAMES = ("chunk", "full", "act", "pool", "mid", "sq")


class Panel:

    def __init__(self, kind, weight, row0, col, chunks=CH, tile0=0, src=None, needs=None):
        self.kind, self.weight, self.row0, self.col = kind, weight, row0, col
        self.chunks, self.tile0, self.src, self.needs = chunks, tile0, src, needs


class Stage:

    def __init__(self, name, iters, panels, index=None, norm=None):
        self.name, self.iters, self.panels, self.norm = name, iters, panels, norm
        self.index = index or (lambda i, k: i * len(panels) + k)


class Counts:

    def __init__(self):
        self.n = {k: 0 for k in NAMES}
        self.i, self.per = None, None

    def at(self, name, more=0):
        v = self.n[name] + more
        return v if self.i is None else self.i * self.per[name] + v

    def enter(self, stage, i):
        self.i = i
        self.start = dict(self.n)
        self.per = {k: 0 for k in NAMES}
        for p in stage.panels:
            self.per["chunk"] += p.chunks
            for k, v in KINDS[p.kind].items():
                self.per[k] += v

    def leave(self, stage):
        self.i = None
        for k in NAMES:
            assert self.n[k] == self.start[k] + self.per[k], (stage.name, k)
            self.n[k] = self.start[k] + stage.iters * self.per[k]

    def event(self, kind):
        for k, v in KINDS[kind].items():
            self.n[k] += v


def make_stages():
    stages = []
    c = Counts()
    ready = {}

    def add(name, iters, panels, makes=None, norm=None, index=None):
        assert norm is None or iters == 1
        stages.append(Stage(name, iters, panels, index, norm))
        made = []
        for i in range(iters):
            for p in panels:
                c.n["chunk"] += p.chunks
                c.event(p.kind)
                if makes and p.kind in makes:
                    made.append(c.n["pool"])
        ready[name] = made
        return made

    for _ in range(CH):
        c.event("x")
    ready["x"] = [c.n["pool"] - CH + 1 + j for j in range(CH)]
    add("q", 1, [Panel("q", "w_qkv", 0, lambda i, g=g: g * PW, src="A", needs="x") for g in range(4)], ("q",))
    kv = []
    o_ready = []
    for g in range(4):
        kv.append(Panel("k", "w_qkv", 0, lambda i, g=g: D + g * PW, src="A"))
        kv.append(Panel("v", "w_qkv", 0, lambda i, g=g: 2 * D + g * PW, src="A"))
    stages.append(Stage("kv", 1, kv))
    for g in range(4):
        for kind in (("k", "v") if g == 0 else ("attn", "k", "v")):
            c.event(kind)
            if kind == "attn":
                o_ready.append(c.n["pool"])
    c.event("attn")
    o_ready.append(c.n["pool"])
    c.n["chunk"] += len(kv) * CH
    ready["kv"] = o_ready
    add("w_o", 1, [Panel("res", "w_o1", 0, lambda i, g=g: g * PW, src="B", needs="kv") for g in range(4)], ("res",))
    for f in range(D_FF // D):
        if f == 0:
            add("w1_0", 1, [Panel("relu2", "w1", 0, lambda i, g=g: g * PW, src="A", needs="w_o") for g in range(4)],
                ("relu2",), norm=0)
        else:
            add(f"w1_{f}", 2, [Panel("relu2", "w1", 0, lambda i, f=f, h=h: f * D + i * 2 * PW + h * PW, src="A",
                                     needs="w_o") for h in range(2)], ("relu2",))
        kind = "res2" if f == D_FF // D - 1 else "add"
        add(f"w2_{f}", 2, [Panel(kind, "w2", f * D, lambda i, h=h: i * 2 * PW + h * PW, src="B", needs=f"w1_{f}")
                           for h in range(2)], (kind,))
    add("u", 1, [Panel(f"u{g}", "w_in", 0, lambda i, g=g: g * PW, src="A", needs="w2_3") for g in range(4)],
        ("u0", "u1", "u2", "u3"), norm=1)

    def loop2(name, kind, weight, col0, src, needs=None, **kw):
        add(name, 2, [Panel(kind, weight, 0, lambda i, h=h: col0 + i * 2 * PW + h * PW, src=src, needs=needs)
                      for h in range(2)], (kind,), **kw)

    loop2("ga", "ga", "w_in", 4 * D, "A")
    add("pw", 1, [Panel("pw", "pool_w", g * PW, lambda i: 0, chunks=1, tile0=g * JT, src="B", needs="u")
                  for g in range(4)])
    loop2("gc", "gc", "w_in", 2 * D, "A")
    loop2("vv", "vv", "w_in", 3 * D, "A")
    loop2("gb", "gb", "w_in", 1 * D, "A")
    loop2("gbr", "gbr", "w_in", 5 * D, "A")
    loop2("co", "co", "conv_out_w", 0, "B", "gb")
    loop2("wo2", "resb", "w_o2", 0, "A", "co")

    def gate_up(name, d, n, j0=0, norm=None):
        return add(name, n, [Panel("gate", "w_gate_up", 0, lambda i: (d + i) * PW, src="B", needs="wo2"),
                             Panel("up", "w_gate_up", 0, lambda i: FFN + (d + i) * PW, src="B", needs="wo2")],
                   ("up",), norm=norm, index=lambda i, k: i + j0)

    done = 0
    for f, n in enumerate((4, 4, 3)):
        if f == 0:
            ready["gu_0"] = gate_up("gu_first", 0, 1, norm=2) + gate_up("gu_rest", 1, n - 1, j0=1)
        else:
            gate_up(f"gu_{f}", done, n)
        if n == 4:
            add(f"dn_{f}", 2, [Panel("add", "w_down", done * PW, lambda i, h=h: i * 2 * PW + h * PW, src="A",
                                     needs=f"gu_{f}") for h in range(2)])
        else:
            add(f"dn_{f}", 1, [Panel("fin", "w_down", done * PW, lambda i, g=g: g * PW, chunks=n, src="A",
                                     needs=f"gu_{f}") for g in range(4)])
        done += n
    return stages, ready, c.n["chunk"]


def build(nc, x, meta, norm_mix, norm_mlp, final_norm, w_qkv, w_o1, w1, w2, norm_mix_2, w_in, b_gate,
          pool_w, pool_scale, conv_w, conv_out_w, w_o2, norm_ffn_2, w_gate_up, w_down, norm_final_2, out):
    stages, ready, n_chunks = make_stages()
    dram = dict(w_qkv=w_qkv[0], w_o1=w_o1[0], w1=w1[0], w2=w2[0], w_in=w_in,
                pool_w=pool_w.rearrange("g c n -> (g c) n"), conv_out_w=conv_out_w, w_o2=w_o2,
                w_gate_up=w_gate_up, w_down=w_down)

    with ExitStack() as ctx:
        top = [(nc.sbuf_base + 63) // 64 * 64]
        arena_bytes = 0

        def place(name, shape, dt=F32, at=None):
            size = 4
            for s in shape[1:]:
                size *= s
            size = (size + 31) // 32 * 32
            off = top[0] if at is None else at
            if at is None:
                top[0] += size
            return nc.alloc_sbuf_tensor_at(name, shape, dt, offset=off), off

        def sem(name):
            return ctx.enter_context(nc.semaphore(name))

        raw, _ = place("raw", [P, RAW, KT, PW])
        whi, _ = place("whi", [P, SPLIT, KT, PW], F32R)
        wlo, _ = place("wlo", [P, SPLIT, KT, PW], F32R)
        a_hi, _ = place("a_hi", [P, NT, TW], F32R)
        a_lo, _ = place("a_lo", [P, NT, TW], F32R)
        b_hi, b_off = place("b_hi", [P, NT, T], F32R)
        b_lo, _ = place("b_lo", [P, NT, T], F32R)
        h, _ = place("h", [P, NT, T])
        full, _ = place("full", [P, JT, T])
        U, u_off = place("U", [P, JT, TW])
        S1, s1_off = place("S1", [P, JT, TW])
        S2, s2_off = place("S2", [P, JT, TW])
        acc, _ = place("acc", [P, JT, T])
        rr, _ = place("rr", [P, TW])
        rr1, _ = place("rr1", [P, T])
        ms, _ = place("ms", [P, 2, TW])
        msum, _ = place("msum", [P, M])
        vec, _ = place("vec", [P, 192])
        ident, _ = place("ident", [P, P])
        ones, _ = place("ones", [P, P])
        negtri, _ = place("negtri", [P, P], F32R)
        negone, _ = place("negone", [P, P], F32R)
        stat, _ = place("stat", [P, 8])
        region = top[0]
        za, _ = place("za", [P, NT, T])
        G, _ = place("G", [P, NT, TW])
        at = region
        k_hi, _ = place("k_hi", [P, JT, T], F32R, at=at)
        k_lo, _ = place("k_lo", [P, JT, T], F32R, at=at + 4096)
        v_hi, _ = place("v_hi", [P, MT, PW], F32R, at=at + 8192)
        v_lo, _ = place("v_lo", [P, MT, PW], F32R, at=at + 12288)
        t1, _ = place("t1", [P, GH, 3 * P], at=at + 16384)
        p_hi, _ = place("p_hi", [P, GH, 3 * P], F32R, at=at + 22528)
        t2, _ = place("t2", [P, GH, 3 * P], at=u_off)
        p_lo, p_off = place("p_lo", [P, GH, 3 * P], F32R, at=at + 28672)
        top[0] = max(top[0], p_off + 4 * GH * 3 * P)
        acc2 = S1[:, :, 0:T]
        sqt = S2[:, :, 0:T]
        x_tok, _ = place("x_tok", [P, MT, D], at=region)
        meta_tok, _ = place("meta_tok", [M, D], at=region + 16384)
        xn_tok, _ = place("xn_tok", [P, MT, D], at=b_off)
        gv, _ = place("gv", [96, 2, P], at=region + 24576)
        tri32, _ = place("tri32", [P, P], at=region + 24576 + 1024)
        o_tok, _ = place("o_tok", [P, MT, D], at=region)
        arena_bytes = top[0] - nc.sbuf_base
        ctx.enter_context(nc.sbuf_tensor("arena", [P, arena_bytes // 4], F32))

        ps = ctx.enter_context(nc.psum_tensor("ps", [P, 8, 512], F32))

        V_MIX, V_MLP, V_FIN1, V_MIX2, V_FFN2, V_FIN2 = (NT * i for i in range(6))
        V_PS, V_BG, V_CV = 96, 96 + NT, 96 + 3 * NT

        raw_landed = [sem(f"raw_landed{s}") for s in range(RAW)]
        w_hi = sem("w_hi")
        w_lo = sem("w_lo")
        w_used = sem("w_used")
        full_ready = sem("full_ready")
        act_done = sem("act_done")
        pool_done = sem("pool_done")
        dve_mid = sem("dve_mid")
        sq_step = sem("sq_step")
        x_landed = sem("x_landed")
        x1_landed = sem("x1_landed")
        vec_landed = sem("vec_landed")
        meta_landed = sem("meta_landed")
        consts = sem("consts")
        tri_ready = sem("tri_ready")
        ssq_ready = sem("ssq_ready")
        ms_ready = sem("ms_ready")
        root_ready = sem("root_ready")
        rstd_ready = sem("rstd_ready")
        xn_ready = sem("xn_ready")
        vec_t = sem("vec_t")
        vec_ready = sem("vec_ready")
        tr_done = sem("tr_done")
        meta_t = sem("meta_t")
        meta_step = sem("meta_step")
        meta_hi = sem("meta_hi")
        norm_mm = sem("norm_mm")
        norm_mid = sem("norm_mid")
        h_scaled = sem("h_scaled")
        z_ready = sem("z_ready")
        z_mid = sem("z_mid")
        z_read = sem("z_read")
        sp_ln = sem("sp_ln")
        sp_raw = sem("sp_raw")
        sp_full = sem("sp_full")
        sp_hi = sem("sp_hi")
        sp_lo = sem("sp_lo")
        arg_ready = sem("arg_ready")
        a_exp = sem("a_exp")
        act_chain = sem("act_chain")
        a_full = sem("a_full")
        aw_hi = sem("aw_hi")
        aw_lo = sem("aw_lo")
        o_ready = sem("o_ready")
        gate_s = sem("gate_s")
        y_t = sem("y_t")
        col_ready = sem("col_ready")
        scaled_dve = sem("scaled_dve")
        scaled_act = sem("scaled_act")
        stored = sem("stored")

        block = ctx.enter_context(nc.Block())

        def cast(ap):
            return ap.bitcast(F32)

        def gain(v0, j):
            return vec[:, bass.ds(v0 + j * JT, JT)].unsqueeze(2).to_broadcast([P, JT, T])

        def rows(r, n):
            return r.unsqueeze(1).to_broadcast([P, JT, n])

        def tiles(buf, j, lo=0, n=T):
            return buf[:, bass.ds(j * JT, JT), lo:lo + n]

        def narrow(half):
            return ps[:, 4 * half:4 * half + 2, :].rearrange("p b (t n) -> p (b t) n", t=2)

        def wide(half):
            return ps[:, 4 * half:4 * half + 4, 0:TW]

        def run(eng, counts, body):
            for st in stages:
                if st.iters == 1:
                    body(st, 0)
                else:
                    with eng.Fori(0, st.iters) as i:
                        counts.enter(st, i)
                        body(st, i)
                    counts.leave(st)

        @block.sync
        def _(sp):
            cnt = Counts()
            sp.dma_start(x_tok[:, 0, :], x[0, 0:P, :]).then_inc(x_landed, 16)
            sp.dma_start(x_tok[:, 1, :], x[0, P:T, :]).then_inc(x1_landed, 16)

            def body(st, i):
                for p in st.panels:
                    src = dram[p.weight]
                    for c in range(p.chunks):
                        n = cnt.n["chunk"]
                        if st.iters > 1 or n >= RAW:
                            sp.wait_ge(w_lo, cnt.at("chunk", 1 - RAW))
                        r = p.row0 + c * KT * P
                        sp.dma_start(raw[:, n % RAW],
                                     src[r:r + KT * P, bass.ds(p.col(i), PW)].rearrange("(t p) n -> p t n", p=P)
                                     ).then_inc(raw_landed[n % RAW], 16)
                        cnt.n["chunk"] += 1

            def loops():
                for st in stages:
                    if st.iters == 1:
                        body(st, 0)
                    else:
                        with sp.Fori(0, st.iters) as i:
                            cnt.i = i
                            start = cnt.n["chunk"]
                            cnt.per = {"chunk": sum(p.chunks for p in st.panels)}
                            body(st, i)
                        cnt.i = None
                        cnt.n["chunk"] = start + st.iters * cnt.per["chunk"]

            loops()
            for half in range(2):
                for m, scaled in ((0, scaled_dve), (1, scaled_act)):
                    cols = slice(half * (D // 2), (half + 1) * (D // 2))
                    sp.wait_ge(scaled, half + 1)
                    sp.dma_start(out[0, m * P:(m + 1) * P, cols], o_tok[:, m, cols]).then_inc(stored, 16)
            sp.wait_ge(stored, 64)

        def landed(eng, n, at):
            eng.wait_ge(raw_landed[n % RAW], at)

        def landed_count(cnt, ahead):
            n = cnt.n["chunk"] + ahead
            base = 16 * (n // RAW + 1)
            if cnt.i is None:
                return base
            assert cnt.per["chunk"] % RAW == 0
            return cnt.i * (16 * cnt.per["chunk"] // RAW) + base

        @block.scalar
        def _(act):
            cnt = Counts()
            for v, r0 in ((norm_mix, V_MIX), (norm_mlp, V_MLP), (final_norm.rearrange("(a d) -> a d", a=1), V_FIN1),
                          (norm_mix_2.rearrange("(a d) -> a d", a=1), V_MIX2),
                          (norm_ffn_2.rearrange("(a d) -> a d", a=1), V_FFN2),
                          (norm_final_2.rearrange("(a d) -> a d", a=1), V_FIN2)):
                act.dma_start(gv[r0:r0 + NT, 0, :], v[0].rearrange("(t p) -> t p", p=P)).then_inc(vec_landed, 16)
            act.dma_start(gv[0:NT, 1, :], pool_scale.rearrange("(t p) -> t p", p=P)).then_inc(vec_landed, 16)
            act.dma_start(gv[NT:3 * NT, 1, :], b_gate.rearrange("(t p) -> t p", p=P)).then_inc(vec_landed, 16)
            act.dma_start(gv[3 * NT:6 * NT, 1, :], conv_w.rearrange("k (t p) -> (k t) p", p=P)).then_inc(vec_landed, 16)
            act.dma_start(meta_tok[:], meta).then_inc(meta_landed, 16)

            def split_hi(ahead=AHEAD):
                n = cnt.n["chunk"] + ahead
                if n >= n_chunks:
                    return
                landed(act, n, landed_count(cnt, ahead))
                if cnt.i is not None or n >= SPLIT:
                    act.wait_ge(w_used, cnt.at("chunk", ahead + 1 - SPLIT))
                act.activation(whi[:, n % SPLIT], raw[:, n % RAW], ACT.Copy).then_inc(w_hi, 1)

            for m, landed_sem in enumerate((x_landed, x1_landed)):
                act.wait_ge(landed_sem, 16)
                act.activation(xn_tok[:, m, :], x_tok[:, m, :], ACT.Square,
                               accum_out=stat[:, m:m + 1]).then_inc(ssq_ready, 1)
            act.wait_ge(ms_ready, 1)
            act.activation(stat[:, 4:6], stat[:, 2:4], ACT.Sqrt).then_inc(root_ready, 1)
            split_hi(0)
            split_hi(1)
            for j in range(CH):
                act.wait_ge(full_ready, cnt.at("full", 1))
                act.activation(tiles(a_hi, j, M), full[:], ACT.Copy).then_inc(act_done, 1)
                cnt.event("x")
            act.wait_ge(meta_step, 2)
            act.activation(a_hi[:, :, 0:M], S1[:, 0, 0:NT * M].rearrange("p (t n) -> p t n", n=M),
                           ACT.Copy).then_inc(meta_hi, 1)

            def evac(kind, j):
                dst = {"q": tiles(b_hi, j), "k": k_hi[:], "v": v_hi[:], "res": tiles(a_hi, j, M),
                       "res2": tiles(a_hi, j, M), "up": tiles(a_hi, j, M), "relu2": tiles(b_hi, j), "co": tiles(a_hi, j, M), "resb": tiles(b_hi, j),
                       "gb": tiles(b_hi, j), "attn": tiles(b_hi, j)}
                if kind in ("u0", "u1", "u2", "u3"):
                    dst[kind] = tiles(b_hi, j)
                if kind == "fin":
                    act.wait_ge(y_t, j + 1)
                    act.activation(o_tok[:, :, j * PW:(j + 1) * PW], ps[:, 2:4, :], ACT.Copy).then_inc(act_done, 1)
                    return
                if not KINDS[kind].get("act"):
                    return
                act.wait_ge(full_ready, cnt.at("full", 1))
                if kind == "ga":
                    act.activation(tiles(za, j), full[:], ACT.Sigmoid).then_inc(act_done, 1)
                elif kind == "gbr":
                    act.activation(tiles(G, j), full[:], ACT.Sigmoid).then_inc(act_done, 1)
                elif kind == "vv":
                    act.activation(tiles(G, j), full[:], ACT.Copy).then_inc(act_done, 1)
                elif kind == "gate":
                    act.activation(S1[:, :, 0:T], U[:, :, 0:T], ACT.Sigmoid).then_inc(act_done, 1)
                else:
                    src = full[:].rearrange("p a b -> p (a b)").rearrange("p (a b) -> p a b", b=PW) if kind == "v" else full[:]
                    act.activation(dst[kind], src, ACT.Copy).then_inc(act_done, 1)

            def root(k):
                act.wait_ge(ms_ready, NORM_AT[k])
                act.activation(ms[:, 1, M:TW], ms[:, 0, M:TW], ACT.Sqrt).then_inc(root_ready, 1)
                if k == 1:
                    act.wait_ge(ms_ready, NORM_AT[k] + 1)
                    act.activation(ms[:, 1, :], ms[:, 0, :], ACT.Sqrt).then_inc(root_ready, 1)

            def weights_exp(g):
                act.wait_ge(arg_ready, g + 1)
                for b, hd in ((2, 0), (6, 2)):
                    last = act.activation(t1[:, hd:hd + 2, :], ps[:, b:b + 2, 0:3 * P], ACT.Exp)
                last.then_inc(a_exp, 1)

            def weights_hi(g):
                act.wait_ge(a_full, g + 1)
                act.activation(p_hi[:], t1[:], ACT.Copy).then_inc(aw_hi, 1)

            def softplus_ln(g):
                act.wait_ge(z_read, g + 1)
                act.activation(t1[:], t1[:], ACT.Exp).then_inc(act_chain, 1)
                act.wait_ge(act_chain, g + 1)
                act.activation(t1[:], t1[:], ACT.Ln, bias=1.0).then_inc(sp_ln, 1)

            def softplus_hi(g):
                act.wait_ge(sp_full, g + 1)
                act.activation(p_hi[:], t2[:], ACT.Copy).then_inc(sp_hi, 1)

            def body(st, i):
                for k, p in enumerate(st.panels):
                    g = k // 2
                    if p.kind == "k" and g > 0:
                        weights_exp(g - 1)
                    if st.name == "w_o" and k == 0:
                        weights_exp(3)
                    for c in range(p.chunks):
                        split_hi()
                        cnt.n["chunk"] += 1
                        if p.kind == "k" and g > 0 or st.name == "w_o" and k == 0:
                            ga = g - 1 if p.kind == "k" else 3
                            if c == 0:
                                weights_hi(ga)
                            if c == 2:
                                evac("attn", ga)
                                cnt.event("attn")
                        if p.kind == "v":
                            if c == 0:
                                softplus_ln(g)
                            if c == 1:
                                softplus_hi(g)
                    if st.norm is not None and k == 0:
                        root(st.norm)
                    evac(p.kind, g if p.kind in "kv" else st.index(i, k))
                    cnt.event(p.kind)

            run(act, cnt, body)
            act.wait_ge(ms_ready, NORM_AT[3])
            act.activation(stat[:, 4:6], stat[:, 2:4], ACT.Sqrt).then_inc(root_ready, 1)
            act.wait_ge(col_ready, 1)
            act.wait_ge(act_done, cnt.at("act"))
            for half in range(2):
                cols = slice(half * (D // 2), (half + 1) * (D // 2))
                act.activation(o_tok[:, 1, cols], o_tok[:, 1, cols], ACT.Copy,
                               scale=stat[:, 1:2]).then_inc(scaled_act, 1)

        @block.vector
        def _(dve):
            cnt = Counts()
            mid = [0]

            def step(ins):
                mid[0] += 1
                ins.then_inc(dve_mid, 1)
                dve.wait_ge(dve_mid, cnt.at("mid", mid[0]))

            def split_lo(ahead=AHEAD):
                n = cnt.n["chunk"] + ahead
                if n >= n_chunks:
                    return
                landed(dve, n, landed_count(cnt, ahead))
                dve.wait_ge(w_hi, cnt.at("chunk", ahead + 1))
                dve.tensor_tensor(wlo[:, n % SPLIT], raw[:, n % RAW], cast(whi[:, n % SPLIT]),
                                  ALU.subtract).then_inc(w_lo, 1)

            dve.memset(ones[:], 1.0)
            dve.memset(acc[:], 0.0).then_inc(consts, 1)
            dve.wait_ge(ssq_ready, 2)
            dve.tensor_scalar(stat[:, 2:4], stat[:, 0:2], 1.0 / D, EPS, ALU.mult, ALU.add).then_inc(ms_ready, 1)
            dve.wait_ge(root_ready, 1)
            dve.reciprocal(stat[:, 6:8], stat[:, 4:6]).then_inc(rstd_ready, 1)
            dve.wait_ge(rstd_ready, 1)
            for m in range(MT):
                dve.tensor_scalar(xn_tok[:, m, :], x_tok[:, m, :], stat[:, 6 + m:7 + m], None,
                                  ALU.mult).then_inc(xn_ready, 1)
            dve.wait_ge(vec_t, 1)
            dve.tensor_copy(vec[:], ps[:, 7, 0:192]).then_inc(vec_ready, 1)
            dve.wait_ge(vec_ready, 1)
            split_lo(0)
            split_lo(1)
            for j in range(CH):
                mid[0] = 0
                dve.wait_ge(tr_done, j + 1)
                if j > 0:
                    dve.wait_ge(pool_done, cnt.at("pool"))
                dve.tensor_copy(tiles(h, j), narrow(0)).then_inc(dve_mid, 1)
                dve.tensor_tensor(full[:], narrow(1), gain(V_MIX, j), ALU.mult).then_inc(full_ready, 1)
                cnt.event("x")
            meta_f = S1[:, 0, 0:NT * M].rearrange("p (t n) -> p t n", n=M)
            dve.wait_ge(meta_t, 1)
            meta_raw = U[:, 0, 0:NT * M]
            dve.tensor_copy(meta_raw, ps[:, 6, 0:NT * M]).then_inc(meta_step, 1)
            dve.wait_ge(meta_step, 1)
            dve.tensor_tensor(meta_f, meta_raw.rearrange("p (t n) -> p t n", n=M),
                              vec[:, V_MIX2:V_MIX2 + NT].unsqueeze(2).to_broadcast([P, NT, M]),
                              ALU.mult).then_inc(meta_step, 1)
            dve.wait_ge(meta_step, 2)
            dve.wait_ge(meta_hi, 1)
            dve.tensor_tensor(a_lo[:, :, 0:M], meta_f, cast(a_hi[:, :, 0:M]), ALU.subtract).then_inc(meta_step, 1)
            dve.tensor_tensor(U[:, 1, 0:NT * M], meta_raw, meta_raw, ALU.mult).then_inc(meta_step, 1)
            dve.wait_ge(meta_step, 4)
            dve.tensor_reduce(msum[:], U[:, 1, 0:NT * M].rearrange("p (t n) -> p n t", n=M), mybir.AxisListType.X,
                              ALU.add).then_inc(meta_step, 1)

            def z_out(g):
                dve.wait_ge(z_ready, g + 1)
                dve.wait_ge(meta_step, 5)
                if g > 0:
                    dve.wait_ge(aw_lo, g)
                for b, hd in ((2, 0), (6, 2)):
                    last = dve.tensor_scalar(t2[:, hd:hd + 2, :], ps[:, b:b + 2, 0:3 * P], 0.0, None, ALU.max)
                last.then_inc(z_mid, 1)
                dve.wait_ge(z_mid, g + 1)
                for b, hd in ((2, 0), (6, 2)):
                    last = dve.scalar_tensor_tensor(out=t1[:, hd:hd + 2, :], in0=t2[:, hd:hd + 2, :], scalar=-2.0,
                                                    in1=ps[:, b:b + 2, 0:3 * P], op0=ALU.mult, op1=ALU.add)
                last.then_inc(z_read, 1)

            def softplus_sum(g):
                dve.wait_ge(sp_ln, g + 1)
                dve.tensor_tensor(t2[:], t2[:], t1[:], ALU.add).then_inc(sp_raw, 1)

            def softplus_lo(g):
                dve.wait_ge(sp_hi, g + 1)
                dve.tensor_tensor(p_lo[:], t2[:], cast(p_hi[:]), ALU.subtract).then_inc(sp_lo, 1)

            def weights_lo(g):
                dve.wait_ge(aw_hi, g + 1)
                dve.tensor_tensor(p_lo[:], t1[:], cast(p_hi[:]), ALU.subtract).then_inc(aw_lo, 1)

            def attn_out(g):
                mid[0] = 0
                dve.wait_ge(o_ready, g + 1)
                dve.wait_ge(pool_done, cnt.at("pool"))
                dve.tensor_copy(full[:, 0:2, :], ps[:, 2:4, 0:T]).then_inc(dve_mid, 1)
                dve.tensor_copy(full[:, 2:4, :], ps[:, 6:8, 0:T]).then_inc(full_ready, 1)
                cnt.event("attn")

            def norm(k):
                dve.wait_ge(norm_mm, k + 1)
                dve.tensor_scalar(ms[:, 0, M:TW], ps[:, 7, 0:T], 1.0 / D, EPS, ALU.mult, ALU.add).then_inc(ms_ready, 1)
                dve.wait_ge(root_ready, NORM_AT[k])
                if k != 1:
                    dve.reciprocal(rr[:, M:TW], ms[:, 1, M:TW]).then_inc(rstd_ready, 1)
                else:
                    dve.reciprocal(rr1[:], ms[:, 1, M:TW]).then_inc(norm_mid, 1)
                    dve.wait_ge(norm_mid, 1)
                    dve.tensor_tensor(ms[:, 0, M:TW], ps[:, 6, M:TW], rr1[:], ALU.mult).then_inc(norm_mid, 1)
                    dve.wait_ge(norm_mid, 2)
                    dve.tensor_tensor(ms[:, 0, M:TW], ms[:, 0, M:TW], rr1[:], ALU.mult)
                    dve.tensor_copy(ms[:, 0, 0:M], ps[:, 6, 0:M]).then_inc(norm_mid, 1)
                    dve.wait_ge(norm_mid, 3)
                    dve.tensor_scalar(ms[:, 0, :], ms[:, 0, :], 1.0 / D, EPS, ALU.mult, ALU.add).then_inc(ms_ready, 1)
                    dve.wait_ge(root_ready, NORM_AT[k] + 1)
                    dve.reciprocal(rr[:], ms[:, 1, :]).then_inc(norm_mid, 1)
                    dve.wait_ge(norm_mid, 4)
                    dve.tensor_tensor(rr[:, M:TW], rr[:, M:TW], rr1[:], ALU.mult).then_inc(rstd_ready, 1)
                dve.wait_ge(rstd_ready, k + 2)

            def evac(kind, half, j):
                mid[0] = 0
                dve.wait_ge(w_used, cnt.at("chunk"))
                dve.wait_ge(full_ready, cnt.at("full"))
                dve.wait_ge(act_done, cnt.at("act"))
                dve.wait_ge(pool_done, cnt.at("pool"))
                n = narrow(half)
                r = rows(rr[:, M:TW], T)
                if kind == "q":
                    last = dve.tensor_scalar(full[:], n, QK_SCALE, None, ALU.mult)
                elif kind in ("k", "v"):
                    last = dve.tensor_copy(full[:], n)
                elif kind == "add":
                    last = dve.tensor_tensor(tiles(h, j), tiles(h, j), n, ALU.add)
                elif kind in ("res", "resb"):
                    step(dve.tensor_tensor(tiles(h, j), tiles(h, j), n, ALU.add))
                    last = dve.tensor_tensor(full[:], tiles(h, j), gain(V_MLP if kind == "res" else V_FFN2, j), ALU.mult)
                elif kind == "res2":
                    dve.wait_ge(sq_step, cnt.at("sq"))
                    step(dve.tensor_tensor(U[:, :, 0:T], tiles(h, j), n, ALU.add))
                    step(dve.tensor_tensor(tiles(h, j), U[:, :, 0:T], gain(V_FIN1, j), ALU.mult))
                    last = dve.tensor_tensor(full[:], tiles(h, j), gain(V_MIX2, j), ALU.mult)
                elif kind == "relu2":
                    step(dve.tensor_tensor(full[:], n, r, ALU.mult))
                    last = dve.scalar_tensor_tensor(out=full[:], in0=full[:], scalar=0.0, in1=full[:],
                                                    op0=ALU.max, op1=ALU.mult)
                elif kind in ("u0", "u1", "u2", "u3"):
                    step(dve.tensor_tensor(U[:], wide(half), rows(rr[:], TW), ALU.mult))
                    src, bufs, w, lo = U, [S1, S2], 1, 0
                    while w < WINDOWS[j]:
                        lo += w
                        dst = bufs[0]
                        step(dve.tensor_tensor(dst[:, :, lo:TW], src[:, :, lo:TW], src[:, :, lo - w:TW - w], ALU.add))
                        src, bufs, w = dst, bufs[::-1], 2 * w
                    last = dve.scalar_tensor_tensor(out=full[:], in0=src[:, :, M:TW], scalar=1.0 / w,
                                                    in1=U[:, :, M:TW], op0=ALU.mult, op1=ALU.subtract)
                elif kind in ("ga", "gbr"):
                    step(dve.tensor_tensor(full[:], n, r, ALU.mult))
                    if kind == "ga":
                        step(dve.tensor_tensor(tiles(h, j), tiles(h, j), rows(rr1[:], T), ALU.mult))
                    last = dve.tensor_tensor(full[:], full[:], gain(V_BG if kind == "ga" else V_BG + NT, j), ALU.add)
                elif kind == "pw":
                    step(dve.tensor_tensor(full[:], n, gain(V_PS, j), ALU.mult))
                    last = dve.tensor_tensor(tiles(za, j), tiles(za, j), full[:], ALU.mult)
                elif kind == "gc":
                    last = dve.tensor_tensor(tiles(G, j, 0, TW), wide(half), rows(rr[:], TW), ALU.mult)
                elif kind == "vv":
                    step(dve.tensor_tensor(U[:], wide(half), rows(rr[:], TW), ALU.mult))
                    step(dve.tensor_tensor(U[:], U[:], tiles(G, j, 0, TW), ALU.mult))
                    for tap in range(3):
                        for t in range(JT):
                            w = vec[:, bass.ds(V_CV + tap * NT + j * JT + t, 1)]
                            v = U[:, t, M - 2 + tap:TW - 2 + tap]
                            if tap == 0:
                                last = dve.tensor_scalar(full[:, t, :], v, w, None, ALU.mult)
                            else:
                                last = dve.scalar_tensor_tensor(out=full[:, t, :], in0=v, scalar=w, in1=full[:, t, :],
                                                                op0=ALU.mult, op1=ALU.add)
                        if tap < 2:
                            step(last)
                elif kind == "gb":
                    step(dve.tensor_tensor(full[:], n, r, ALU.mult))
                    last = dve.tensor_tensor(full[:], full[:], tiles(G, j), ALU.mult)
                elif kind == "co":
                    step(dve.tensor_tensor(full[:], n, tiles(G, j), ALU.mult))
                    last = dve.tensor_tensor(full[:], full[:], tiles(za, j), ALU.add)
                elif kind == "gate":
                    last = dve.tensor_tensor(U[:, :, 0:T], n, r, ALU.mult)
                elif kind == "up":
                    step(dve.tensor_tensor(full[:], n, r, ALU.mult))
                    last = dve.tensor_tensor(full[:], full[:], S1[:, :, 0:T], ALU.mult)
                elif kind == "fin":
                    dve.wait_ge(sq_step, cnt.at("sq"))
                    step(dve.tensor_tensor(tiles(h, j), tiles(h, j), n, ALU.add))
                    if j > 0:
                        dve.wait_ge(y_t, j)
                    last = dve.tensor_tensor(full[:], tiles(h, j), gain(V_FIN2, j), ALU.mult)
                last.then_inc(full_ready, 1)

            def body(st, i):
                for k, p in enumerate(st.panels):
                    g = k // 2
                    for c in range(p.chunks):
                        if c == 3 and (p.kind == "k" and g > 0 or st.name == "w_o" and k == 0):
                            attn_out(g - 1 if p.kind == "k" else 3)
                        split_lo()
                        cnt.n["chunk"] += 1
                        if c == 0 and (p.kind == "k" and g > 0 or st.name == "w_o" and k == 0):
                            weights_lo(g - 1 if p.kind == "k" else 3)
                        if p.kind == "v":
                            if c == 0:
                                z_out(g)
                            if c == 1:
                                softplus_sum(g)
                            if c == 2:
                                softplus_lo(g)
                    if st.norm is not None and k == 0:
                        norm(st.norm)
                    evac(p.kind, k % 2, g if p.kind in ("k", "v") else st.index(i, k))
                    cnt.event(p.kind)

            run(dve, cnt, body)
            dve.wait_ge(norm_mm, 4)
            dve.tensor_scalar(stat[:, 2:4], ps[:, 7, 0:4].rearrange("p (m n) -> p m n", n=2)[:, :, 0], 1.0 / D, EPS,
                              ALU.mult, ALU.add).then_inc(ms_ready, 1)
            dve.wait_ge(root_ready, NORM_AT[3])
            dve.reciprocal(stat[:, 0:2], stat[:, 4:6]).then_inc(col_ready, 1)
            dve.wait_ge(col_ready, 1)
            dve.wait_ge(act_done, cnt.at("act"))
            for half in range(2):
                cols = slice(half * (D // 2), (half + 1) * (D // 2))
                dve.tensor_scalar(o_tok[:, 0, cols], o_tok[:, 0, cols], stat[:, 0:1], None,
                                  ALU.mult).then_inc(scaled_dve, 1)

        @block.gpsimd
        def _(pool):
            cnt = Counts()
            pool.memset(ident[:], 0.0).then_inc(tri_ready, 1)
            pool.wait_ge(tri_ready, 1)
            pool.affine_select(out=ident[:], in_=ident[:], compare_op=ALU.not_equal, fill=1.0, base=0,
                               pattern=[[-1, P]], channel_multiplier=1).then_inc(consts, 1)
            pool.memset(tri32[:], -1.0).then_inc(tri_ready, 1)
            pool.wait_ge(tri_ready, 2)
            pool.tensor_copy(negone[:], tri32[:]).then_inc(tri_ready, 1)
            pool.wait_ge(tri_ready, 3)
            pool.affine_select(out=tri32[:], in_=tri32[:], compare_op=ALU.is_ge, fill=0.0, base=0,
                               pattern=[[-1, P]], channel_multiplier=1).then_inc(tri_ready, 1)
            pool.wait_ge(tri_ready, 4)
            pool.tensor_copy(negtri[:], tri32[:]).then_inc(tri_ready, 1)
            for j in range(CH):
                pool.wait_ge(act_done, cnt.at("act", 1))
                pool.tensor_tensor(tiles(a_lo, j, M), full[:], cast(tiles(a_hi, j, M)),
                                   ALU.subtract).then_inc(pool_done, 1)
                cnt.event("x")

            def lo_part(kind, j):
                pairs = {"q": ("b", tiles), "relu2": ("b", tiles), "gb": ("b", tiles), "attn": ("b", tiles), "resb": ("b", tiles),
                         "u0": ("b", tiles), "u1": ("b", tiles), "u2": ("b", tiles), "u3": ("b", tiles)}
                if kind == "k":
                    lo, hi, src = k_lo[:], k_hi[:], full[:]
                elif kind == "v":
                    lo, hi = v_lo[:], v_hi[:]
                    src = full[:].rearrange("p a b -> p (a b)").rearrange("p (a b) -> p a b", b=PW)
                elif kind in pairs:
                    lo, hi, src = tiles(b_lo, j), tiles(b_hi, j), full[:]
                else:
                    lo, hi, src = tiles(a_lo, j, M), tiles(a_hi, j, M), full[:]
                pool.wait_ge(act_done, cnt.at("act", 1))
                pool.tensor_tensor(lo, src, cast(hi), ALU.subtract).then_inc(pool_done, 1)

            def add_squares(src, dst, n):
                pool.tensor_tensor(sqt, src, src, ALU.mult).then_inc(sq_step, 1)
                pool.wait_ge(sq_step, cnt.at("sq", n + 1))
                pool.tensor_tensor(dst, dst, sqt, ALU.add).then_inc(sq_step, 1)
                pool.wait_ge(sq_step, cnt.at("sq", n + 2))

            def mask(t, before, after, g):
                pool.wait_ge(before, g + 1)
                for hd in range(GH):
                    v = t[:, hd, :].rearrange("p (b n) -> p b n", n=P)[:, 0:3:2, :]
                    last = pool.affine_select(out=v, in_=v, compare_op=ALU.is_gt, fill=0.0, base=0,
                                              pattern=[[0, 2], [1, P]], channel_multiplier=-1)
                last.then_inc(after, 1)

            def evac(kind, j):
                if kind in ("res", "resb", "res2", "fin"):
                    pool.wait_ge(full_ready, cnt.at("full", 1))
                    if kind == "res2":
                        add_squares(U[:, :, 0:T], acc[:], 0)
                        add_squares(tiles(h, j), acc2, 2)
                    else:
                        add_squares(tiles(h, j), acc[:], 0)
                if kind == "gate":
                    pool.wait_ge(act_done, cnt.at("act", 1))
                    pool.tensor_tensor(S1[:, :, 0:T], S1[:, :, 0:T], U[:, :, 0:T], ALU.mult).then_inc(pool_done, 1)
                elif KINDS[kind].get("pool"):
                    lo_part(kind, j)

            def body(st, i):
                for k, p in enumerate(st.panels):
                    g = k // 2
                    for c in range(p.chunks):
                        cnt.n["chunk"] += 1
                        if p.kind == "k" and g > 0 or st.name == "w_o" and k == 0:
                            ga = g - 1 if p.kind == "k" else 3
                            if c == 0:
                                mask(t1, a_exp, a_full, ga)
                            if c == 2:
                                lo_part("attn", ga)
                                cnt.event("attn")
                        if p.kind == "v" and c == 0:
                            mask(t2, sp_raw, sp_full, g)
                    evac(p.kind, g if p.kind in ("k", "v") else st.index(i, k))
                    cnt.event(p.kind)

            def fresh_sums(norms):
                pool.wait_ge(norm_mm, norms)
                if norms == 1:
                    pool.memset(acc2, 0.0)
                pool.memset(acc[:], 0.0).then_inc(tri_ready, 1)
                pool.wait_ge(tri_ready, 5 + norms)

            pool.wait_ge(consts, 2)
            for st in stages:
                if st.name in ("w2_3", "wo2", "dn_2"):
                    fresh_sums({"w2_3": 1, "wo2": 2, "dn_2": 3}[st.name])
                if st.iters == 1:
                    body(st, 0)
                else:
                    with pool.Fori(0, st.iters) as i:
                        cnt.enter(st, i)
                        body(st, i)
                    cnt.leave(st)

        @block.tensor
        def _(pe):
            cnt = Counts()
            pe.wait_ge(consts, 2)
            pe.wait_ge(vec_landed, 16 * 9)
            for b in range(2):
                last = pe.transpose(ps[:, 7, 96 * b:96 * b + 96], gv[:, b, :], ident[0:96, 0:96])
            last.then_inc(vec_t, 1)
            pe.wait_ge(meta_landed, 16)
            for t in range(NT):
                last = pe.transpose(ps[:, 6, t * M:(t + 1) * M], meta_tok[:, t * P:(t + 1) * P], ident[0:M, 0:M])
            last.then_inc(meta_t, 1)
            pe.wait_ge(x_landed, 16)
            pe.wait_ge(x1_landed, 16)
            pe.wait_ge(xn_ready, 2)
            for j in range(CH):
                if j > 0:
                    pe.wait_ge(full_ready, j)
                for half, src in ((0, x_tok), (1, xn_tok)):
                    for t in range(JT):
                        for m in range(MT):
                            last = pe.transpose(narrow(half)[:, t, m * P:(m + 1) * P],
                                                src[:, m, (j * JT + t) * P:(j * JT + t + 1) * P], ident[:])
                last.then_inc(tr_done, 1)
                cnt.event("x")

            bufs = {"A": (a_hi, a_lo, M), "B": (b_hi, b_lo, 0)}

            def three(out, w_h, w_l, x_h, x_l, start, stop):
                pe.matmul(out, w_h, x_h, start=start, stop=False, skip_group_check=True)
                pe.matmul(out, w_h, x_l, start=False, stop=False, skip_group_check=True)
                return pe.matmul(out, w_l, x_h, start=False, stop=stop, skip_group_check=True)

            def chunk(p, c, half):
                n = cnt.n["chunk"]
                s = n % SPLIT
                pe.wait_ge(w_lo, cnt.at("chunk", 1))
                if p.needs:
                    pe.wait_ge(pool_done, ready[p.needs][c if p.chunks > 1 else p.tile0 // JT])
                hi, lo, off = bufs[p.src]
                for j in range(JT):
                    for kt in range(KT):
                        x = p.tile0 + c * KT + kt
                        first = c == 0 and kt == 0
                        stop = c == p.chunks - 1 and kt == KT - 1
                        if p.kind == "v":
                            if j >= MT:
                                break
                            tok = slice(off + j * P, off + (j + 1) * P)
                            last = three(ps[:, 4 * half + j, :], hi[:, x, tok], lo[:, x, tok],
                                         whi[:, s, kt, :], wlo[:, s, kt, :], first, stop)
                            continue
                        cols = slice(j * P, (j + 1) * P)
                        if p.kind in WIDE:
                            o, tok = ps[:, 4 * half + j, 0:TW], slice(0, TW)
                        else:
                            o, tok = ps[:, 4 * half + j // 2, (j % 2) * T:(j % 2 + 1) * T], slice(off, off + T)
                            first = first and j % 2 == 0
                        last = three(o, whi[:, s, kt, cols], wlo[:, s, kt, cols], hi[:, x, tok], lo[:, x, tok],
                                     first, stop)
                last.then_inc(w_used, 1)
                cnt.n["chunk"] += 1

            hb = (2, 3, 6, 7)

            def scores(g):
                pe.wait_ge(pool_done, cnt.at("pool"))
                for hd in range(GH):
                    t = g * GH + hd
                    three(ps[:, hb[hd], 0:T], k_hi[:, hd, 0:P], k_lo[:, hd, 0:P], b_hi[:, t, :], b_lo[:, t, :],
                          True, False)
                    last = three(ps[:, hb[hd], T:T + P], k_hi[:, hd, P:T], k_lo[:, hd, P:T],
                                 b_hi[:, t, P:T], b_lo[:, t, P:T], False, False)
                last.then_inc(z_ready, 1)

            def suffix_sums(g):
                pe.wait_ge(sp_lo, g + 1)
                pe.wait_ge(tri_ready, 5)
                for hd in range(GH):
                    for part in (p_hi, p_lo):
                        pe.matmul(ps[:, hb[hd], 0:T], negtri[:], part[:, hd, 0:T], start=False, stop=False,
                                  skip_group_check=True)
                        pe.matmul(ps[:, hb[hd], P:T], negone[:], part[:, hd, T:T + P], start=False, stop=False,
                                  skip_group_check=True)
                        last = pe.matmul(ps[:, hb[hd], T:T + P], negtri[:], part[:, hd, T:T + P], start=False,
                                         stop=part is p_lo, skip_group_check=True)
                last.then_inc(arg_ready, 1)

            def values(g):
                pe.wait_ge(aw_lo, g + 1)
                for hd in range(GH):
                    col = slice(hd * HD, (hd + 1) * HD)
                    three(ps[:, hb[hd], 0:T], v_hi[:, 0, col], v_lo[:, 0, col], p_hi[:, hd, 0:T], p_lo[:, hd, 0:T],
                          True, False)
                    last = three(ps[:, hb[hd], P:T], v_hi[:, 1, col], v_lo[:, 1, col], p_hi[:, hd, T:T + P],
                                 p_lo[:, hd, T:T + P], False, True)
                last.then_inc(o_ready, 1)

            def norm(k):
                pe.wait_ge(sq_step, cnt.n["sq"])
                for s in range(JT):
                    last = pe.matmul(ps[:, 7, 0:T], ones[:], acc[:, s, :], start=(s == 0), stop=(s == JT - 1),
                                     skip_group_check=True)
                if k == 1:
                    pe.wait_ge(meta_step, 5)
                    pe.matmul(ps[:, 6, 0:M], ones[:], msum[:], start=True, stop=True, skip_group_check=True)
                    for s in range(JT):
                        last = pe.matmul(ps[:, 6, M:TW], ones[:], acc2[:, s, :], start=False, stop=(s == JT - 1),
                                         skip_group_check=True)
                last.then_inc(norm_mm, 1)

            def turn(j):
                pe.wait_ge(full_ready, cnt.at("full"))
                if j > 0:
                    pe.wait_ge(act_done, cnt.at("act", -1))
                for m in range(MT):
                    for t in range(JT):
                        last = pe.transpose(ps[:, 2 + m, t * P:(t + 1) * P], full[:, t, m * P:(m + 1) * P], ident[:])
                last.then_inc(y_t, 1)

            def body(st, i):
                for k, p in enumerate(st.panels):
                    g = k // 2
                    back = 0 if st.name == "q" and k < 2 else -2 if st.name == "kv" and k > 1 or st.name == "w_o" and k < 2 else -1
                    if st.name == "w_o" and k == 0:
                        cnt.event("attn")
                    pe.wait_ge(full_ready, cnt.at("full", back))
                    if st.name == "u" and k == 0:
                        pe.wait_ge(meta_step, 5)
                    if st.name == "u" and k == 1:
                        pe.wait_ge(rstd_ready, 3)
                    for c in range(p.chunks):
                        chunk(p, c, k % 2)
                        if c == 2 and p.kind == "k" and g > 0:
                            values(g - 1)
                        if c == 1 and st.name == "w_o" and k == 0:
                            values(3)
                        if c == 0 and p.kind == "v":
                            scores(g)
                        if c == 3 and p.kind == "v":
                            suffix_sums(g)
                        if c == 0 and st.name == "dn_2" and k > 0:
                            turn(k - 1)
                    if st.norm is not None and k == 0:
                        norm(st.norm)
                    cnt.event(p.kind)
                    if st.name == "kv" and p.kind == "v" and g < 3:
                        cnt.event("attn")

            run(pe, cnt, body)
            turn(3)
            pe.wait_ge(sq_step, cnt.n["sq"])
            for m in range(MT):
                for s in range(JT):
                    last = pe.matmul(ps[:, 7, 2 * m:2 * m + 2], acc[:, s, m * P:(m + 1) * P], ones[:, 0:2],
                                     start=(m == 0 and s == 0), stop=(s == JT - 1), skip_group_check=True)
            last.then_inc(norm_mm, 1)


_INS = ["x", "meta_tokens_2", "norm_mix", "norm_mlp", "final_norm", "sb_w_qkv", "sb_w_o", "mlp_w1", "mlp_w2",
        "norm_mix_g_2", "w_in_2", "b_gate_2", "pool_w_2", "pool_scale_2", "conv_w_2", "conv_out_w_2", "w_o_2",
        "norm_ffn_g_2", "w_gate_up_2", "w_down_2", "norm_final_g_2"]


def kernel(**inputs):
    import numpy as np
    import concourse.bacc as bacc
    from concourse.bass_utils import run_bass_kernel_spmd

    nc = bacc.Bacc("TRN2", target_bir_lowering=False, num_devices=1)
    arrays, args = {}, []
    for name in _INS:
        a = np.ascontiguousarray(inputs[name])
        arrays[f"in_{name}_dram"] = a
        args.append(nc.dram_tensor(f"in_{name}_dram", a.shape, mybir.dt.from_np(a.dtype), kind="ExternalInput").ap())
    out = nc.dram_tensor("out_dram", (1, T, D), F32, kind="ExternalOutput").ap()
    build(nc, *args, out)
    r = run_bass_kernel_spmd(nc, [arrays], core_ids=[0])
    return r.results[0]["out_dram"]
```

```python
from contextlib import ExitStack

import concourse.bass as bass
from concourse import mybir

ALU = mybir.AluOpType
ACT = mybir.ActivationFunctionType
F32 = mybir.dt.float32
F32R = mybir.dt.float32r

P = 128
D = 2048
NT = D // P
T = 256
MT = T // P
M = 16
TW = M + T
HD = 128
HEADS = D // HD
GH = 4
KT = 4
PW = 512
JT = PW // P
CH = D // (KT * P)
D_FF = 4 * D
FFN = 5632
WINDOWS = (2, 4, 8, 16)
EPS = 1e-6
QK_SCALE = HD ** -0.5
RAW = 4
UK = 2
UNITS = KT // UK
SPLIT = 4
AHEAD = SPLIT

KINDS = {
    "x": dict(full=1, act=2, pool=1),
    "q": dict(full=1, act=1, pool=1),
    "k": dict(full=1, act=1, pool=1),
    "v": dict(full=1, act=1, pool=1),
    "attn": dict(full=1, act=1, pool=1, mid=1),
    "res": dict(full=1, act=2, pool=1, mid=1, sq=1),
    "resb": dict(full=1, act=2, pool=1, mid=1, sq=1),
    "res2": dict(full=1, act=3, pool=1, mid=2, sq=2),
    "add": dict(full=1),
    "relu2": dict(full=1, act=1, pool=1, mid=1),
    "u0": dict(full=1, pool=2, mid=2),
    "u1": dict(full=1, pool=2, mid=3),
    "u2": dict(full=1, pool=2, mid=4),
    "u3": dict(full=1, pool=2, mid=5),
    "ga": dict(full=1, act=1, mid=2),
    "pw": dict(full=1, mid=1),
    "gc": dict(full=1),
    "vv": dict(full=1, pool=5, mid=1),
    "gb": dict(full=1, act=1, pool=1, mid=1),
    "gbr": dict(full=1, act=1, mid=1),
    "co": dict(full=1, act=1, pool=1, mid=1),
    "gate": dict(full=1, act=1, pool=1),
    "up": dict(full=1, act=1, pool=1, mid=1),
    "fin": dict(full=1, act=2, mid=1),
}
WIDE = ("u0", "u1", "u2", "u3", "gc", "vv")
NORM_AT = (2, 3, 5, 6)
NORM_CHUNK = 2
NAMES = ("chunk", "full", "act", "pool", "mid", "sq")


class Panel:

    def __init__(self, kind, weight, row0, col, chunks=CH, tile0=0, src=None, needs=None):
        self.kind, self.weight, self.row0, self.col = kind, weight, row0, col
        self.chunks, self.tile0, self.src, self.needs = chunks, tile0, src, needs


class Stage:

    def __init__(self, name, iters, panels, index=None, norm=None, order=None, attn=None):
        self.name, self.iters, self.panels, self.norm = name, iters, panels, norm
        self.order = order or [(k, c) for k, p in enumerate(panels) for c in range(p.chunks)]
        self.attn = attn
        self.index = index or (lambda i, k: i * len(panels) + k)


def attn_steps(st, q):
    if st.attn is None:
        return []
    steps = [(g, st.attn + q - (8 * g + 4)) for g in range(HEADS // GH)]
    return [(g, s) for g, s in steps if 0 <= s <= 8]


class Counts:

    def __init__(self):
        self.n = {k: 0 for k in NAMES}
        self.i, self.per = None, None

    def at(self, name, more=0):
        v = self.n[name] + more
        return v if self.i is None else self.i * self.per[name] + v

    def enter(self, stage, i):
        self.i = i
        self.start = dict(self.n)
        self.per = {k: 0 for k in NAMES}
        for p in stage.panels:
            self.per["chunk"] += p.chunks
            for k, v in KINDS[p.kind].items():
                self.per[k] += v

    def leave(self, stage):
        self.i = None
        for k in NAMES:
            assert self.n[k] == self.start[k] + self.per[k], (stage.name, k)
            self.n[k] = self.start[k] + stage.iters * self.per[k]

    def event(self, kind):
        for k, v in KINDS[kind].items():
            self.n[k] += v


def make_stages():
    stages = []
    c = Counts()
    ready = {}

    def add(name, iters, panels, makes=None, norm=None, index=None):
        assert norm is None or iters == 1
        stages.append(Stage(name, iters, panels, index, norm))
        made = []
        for i in range(iters):
            for p in panels:
                c.n["chunk"] += p.chunks
                c.event(p.kind)
                if makes and p.kind in makes:
                    made.append(c.n["pool"])
        ready[name] = made
        return made

    for _ in range(CH):
        c.event("x")
    ready["x"] = [c.n["pool"] - CH + 1 + j for j in range(CH)]
    add("q", 1, [Panel("q", "w_qkv", 0, lambda i, g=g: g * PW, src="A", needs="x") for g in range(4)], ("q",))
    kv = []
    o_ready = []
    for g in range(4):
        kv.append(Panel("k", "w_qkv", 0, lambda i, g=g: D + g * PW, src="A"))
        kv.append(Panel("v", "w_qkv", 0, lambda i, g=g: 2 * D + g * PW, src="A"))
    stages.append(Stage("kv", 1, kv, attn=0))
    for kind in ("k", "v", "k", "attn", "v", "k", "attn", "v", "k", "attn", "v", "attn"):
        c.event(kind)
        if kind == "attn":
            o_ready.append(c.n["pool"])
    c.n["chunk"] += len(kv) * CH
    ready["kv"] = o_ready
    add("w_o", 1, [Panel("res", "w_o1", 0, lambda i, g=g: g * PW, src="B", needs="kv") for g in range(4)], ("res",))
    stages[-1].order = ([(0, 0), (0, 1), (0, 2), (1, 0), (1, 1), (1, 2), (0, 3), (1, 3)] +
                        [(k, ch) for k in (2, 3) for ch in range(CH)])
    stages[-1].attn = len(kv) * CH
    for f in range(D_FF // D):
        if f == 0:
            add("w1_0", 1, [Panel("relu2", "w1", 0, lambda i, g=g: g * PW, src="A", needs="w_o") for g in range(4)],
                ("relu2",), norm=0)
        else:
            add(f"w1_{f}", 2, [Panel("relu2", "w1", 0, lambda i, f=f, h=h: f * D + i * 2 * PW + h * PW, src="A",
                                     needs="w_o") for h in range(2)], ("relu2",))
        kind = "res2" if f == D_FF // D - 1 else "add"
        add(f"w2_{f}", 2, [Panel(kind, "w2", f * D, lambda i, h=h: i * 2 * PW + h * PW, src="B", needs=f"w1_{f}")
                           for h in range(2)], (kind,))
    add("u", 1, [Panel(f"u{g}", "w_in", 0, lambda i, g=g: g * PW, src="A", needs="w2_3") for g in range(4)],
        ("u0", "u1", "u2", "u3"), norm=1)

    def loop2(name, kind, weight, col0, src, needs=None, **kw):
        add(name, 2, [Panel(kind, weight, 0, lambda i, h=h: col0 + i * 2 * PW + h * PW, src=src, needs=needs)
                      for h in range(2)], (kind,), **kw)

    loop2("ga", "ga", "w_in", 4 * D, "A")
    add("pw", 1, [Panel("pw", "pool_w", g * PW, lambda i: 0, chunks=1, tile0=g * JT, src="B", needs="u")
                  for g in range(4)])
    loop2("gc", "gc", "w_in", 2 * D, "A")
    loop2("vv", "vv", "w_in", 3 * D, "A")
    loop2("gb", "gb", "w_in", 1 * D, "A")
    loop2("gbr", "gbr", "w_in", 5 * D, "A")
    loop2("co", "co", "conv_out_w", 0, "B", "gb")
    loop2("wo2", "resb", "w_o2", 0, "A", "co")

    def gate_up(name, d, n, j0=0, norm=None):
        return add(name, n, [Panel("gate", "w_gate_up", 0, lambda i: (d + i) * PW, src="B", needs="wo2"),
                             Panel("up", "w_gate_up", 0, lambda i: FFN + (d + i) * PW, src="B", needs="wo2")],
                   ("up",), norm=norm, index=lambda i, k: i + j0)

    done = 0
    for f, n in enumerate((4, 4, 3)):
        if f == 0:
            ready["gu_0"] = gate_up("gu_first", 0, 1, norm=2) + gate_up("gu_rest", 1, n - 1, j0=1)
        else:
            gate_up(f"gu_{f}", done, n)
        if n == 4:
            add(f"dn_{f}", 2, [Panel("add", "w_down", done * PW, lambda i, h=h: i * 2 * PW + h * PW, src="A",
                                     needs=f"gu_{f}") for h in range(2)])
        else:
            add(f"dn_{f}", 1, [Panel("fin", "w_down", done * PW, lambda i, g=g: g * PW, chunks=n, src="A",
                                     needs=f"gu_{f}") for g in range(4)])
        done += n
    return stages, ready, c.n["chunk"]


def build(nc, x, meta, norm_mix, norm_mlp, final_norm, w_qkv, w_o1, w1, w2, norm_mix_2, w_in, b_gate,
          pool_w, pool_scale, conv_w, conv_out_w, w_o2, norm_ffn_2, w_gate_up, w_down, norm_final_2, out):
    stages, ready, n_chunks = make_stages()
    dram = dict(w_qkv=w_qkv[0], w_o1=w_o1[0], w1=w1[0], w2=w2[0], w_in=w_in,
                pool_w=pool_w.rearrange("g c n -> (g c) n"), conv_out_w=conv_out_w, w_o2=w_o2,
                w_gate_up=w_gate_up, w_down=w_down)

    with ExitStack() as ctx:
        top = [(nc.sbuf_base + 63) // 64 * 64]
        arena_bytes = 0

        def place(name, shape, dt=F32, at=None):
            size = 4
            for s in shape[1:]:
                size *= s
            size = (size + 31) // 32 * 32
            off = top[0] if at is None else at
            if at is None:
                top[0] += size
            return nc.alloc_sbuf_tensor_at(name, shape, dt, offset=off), off

        def sem(name):
            return ctx.enter_context(nc.semaphore(name))

        raw, _ = place("raw", [P, RAW, KT, PW])
        whi, _ = place("whi", [P, SPLIT, UK, PW], F32R)
        wlo, _ = place("wlo", [P, SPLIT, UK, PW], F32R)
        a_hi, _ = place("a_hi", [P, NT, TW], F32R)
        a_lo, _ = place("a_lo", [P, NT, TW], F32R)
        b_hi, b_off = place("b_hi", [P, NT, T], F32R)
        b_lo, _ = place("b_lo", [P, NT, T], F32R)
        h, _ = place("h", [P, NT, T])
        full, _ = place("full", [P, JT, T])
        U, u_off = place("U", [P, JT, TW])
        S1, s1_off = place("S1", [P, JT, TW])
        S2, s2_off = place("S2", [P, JT, TW])
        acc, _ = place("acc", [P, JT, T])
        rr, _ = place("rr", [P, TW])
        rr1, _ = place("rr1", [P, T])
        ms, _ = place("ms", [P, 2, TW])
        msum, _ = place("msum", [P, M])
        vec, _ = place("vec", [P, 192])
        ident, _ = place("ident", [P, P])
        ones, _ = place("ones", [P, P])
        negtri, _ = place("negtri", [P, P], F32R)
        negone, _ = place("negone", [P, P], F32R)
        stat, _ = place("stat", [P, 8])
        region = top[0]
        za, _ = place("za", [P, NT, T])
        G, _ = place("G", [P, NT, TW])
        at = region
        k_hi, _ = place("k_hi", [P, JT, T], F32R, at=at)
        k_lo, _ = place("k_lo", [P, JT, T], F32R, at=at + 4096)
        v_hi, _ = place("v_hi", [P, MT, PW], F32R, at=at + 8192)
        v_lo, _ = place("v_lo", [P, MT, PW], F32R, at=at + 12288)
        t1, _ = place("t1", [P, GH, 3 * P], at=at + 16384)
        p_hi, _ = place("p_hi", [P, GH, 3 * P], F32R, at=at + 22528)
        t2, _ = place("t2", [P, GH, 3 * P], at=u_off)
        p_lo, p_off = place("p_lo", [P, GH, 3 * P], F32R, at=at + 28672)
        top[0] = max(top[0], p_off + 4 * GH * 3 * P)
        acc2 = S1[:, :, 0:T]
        sqt = S2[:, :, 0:T]
        x_tok, _ = place("x_tok", [P, MT, D], at=region)
        meta_tok, _ = place("meta_tok", [M, D], at=region + 16384)
        x_sq, _ = place("x_sq", [P, D], at=b_off)
        gv, _ = place("gv", [96, 2, P], at=region + 24576)
        tri32, _ = place("tri32", [P, P], at=region + 24576 + 1024)
        o_tok, _ = place("o_tok", [P, MT, D], at=region)
        arena_bytes = top[0] - nc.sbuf_base
        ctx.enter_context(nc.sbuf_tensor("arena", [P, arena_bytes // 4], F32))

        ps = ctx.enter_context(nc.psum_tensor("ps", [P, 8, 512], F32))

        V_MIX, V_MLP, V_FIN1, V_MIX2, V_FFN2, V_FIN2 = (NT * i for i in range(6))
        V_PS, V_BG, V_CV = 96, 96 + NT, 96 + 3 * NT

        raw_landed = [sem(f"raw_landed{s}") for s in range(RAW)]
        w_hi = sem("w_hi")
        w_lo = sem("w_lo")
        w_used = sem("w_used")
        full_ready = sem("full_ready")
        act_done = sem("act_done")
        pool_done = sem("pool_done")
        dve_mid = sem("dve_mid")
        sq_step = sem("sq_step")
        x_landed = [sem(f"x_landed{j}") for j in range(CH)]
        vec_landed = sem("vec_landed")
        meta_landed = sem("meta_landed")
        consts = sem("consts")
        tri_ready = sem("tri_ready")
        ssq_ready = sem("ssq_ready")
        ms_ready = sem("ms_ready")
        root_ready = sem("root_ready")
        rstd_ready = sem("rstd_ready")
        diag_ready = sem("diag_ready")
        rr_mm = sem("rr_mm")
        vec_t = sem("vec_t")
        vec_ready = sem("vec_ready")
        tr_done = sem("tr_done")
        meta_t = sem("meta_t")
        meta_step = sem("meta_step")
        meta_hi = sem("meta_hi")
        norm_mm = sem("norm_mm")
        norm_mid = sem("norm_mid")
        h_scaled = sem("h_scaled")
        z_ready = sem("z_ready")
        z_mid = sem("z_mid")
        z_read = sem("z_read")
        sp_ln = sem("sp_ln")
        sp_raw = sem("sp_raw")
        sp_full = sem("sp_full")
        sp_hi = sem("sp_hi")
        sp_lo = sem("sp_lo")
        arg_ready = sem("arg_ready")
        a_exp = sem("a_exp")
        act_chain = sem("act_chain")
        a_full = sem("a_full")
        aw_hi = sem("aw_hi")
        aw_lo = sem("aw_lo")
        o_ready = sem("o_ready")
        gate_s = sem("gate_s")
        y_t = sem("y_t")
        col_ready = sem("col_ready")
        scaled_dve = sem("scaled_dve")
        scaled_act = sem("scaled_act")
        stored = sem("stored")

        block = ctx.enter_context(nc.Block())

        def cast(ap):
            return ap.bitcast(F32)

        def gain(v0, j):
            return vec[:, bass.ds(v0 + j * JT, JT)].unsqueeze(2).to_broadcast([P, JT, T])

        def rows(r, n):
            return r.unsqueeze(1).to_broadcast([P, JT, n])

        def tiles(buf, j, lo=0, n=T):
            return buf[:, bass.ds(j * JT, JT), lo:lo + n]

        def narrow(half):
            return ps[:, 4 * half:4 * half + 2, :].rearrange("p b (t n) -> p (b t) n", t=2)

        def wide(half):
            return ps[:, 4 * half:4 * half + 4, 0:TW]

        def x_bank(j):
            return ps[:, 2 + 4 * (j % 2):4 + 4 * (j % 2), :].rearrange("p b (t n) -> p (b t) n", t=2)

        def run(eng, counts, body):
            for st in stages:
                if st.iters == 1:
                    body(st, 0)
                else:
                    with eng.Fori(0, st.iters) as i:
                        counts.enter(st, i)
                        body(st, i)
                    counts.leave(st)

        @block.sync
        def _(sp):
            cnt = Counts()

            def load_x(j):
                cols = slice(j * PW, (j + 1) * PW)
                sp.dma_start(x_tok[:, :, cols], x[0, :, cols].rearrange("(m p) n -> p m n", p=P)
                             ).then_inc(x_landed[j], 16)

            load_x(0)
            load_x(1)

            def body(st, i):
                for k, c in st.order:
                    p = st.panels[k]
                    src = dram[p.weight]
                    n = cnt.n["chunk"]
                    if n == 1:
                        load_x(2)
                        load_x(3)
                    if st.iters > 1 or n >= RAW:
                        sp.wait_ge(w_lo, cnt.at("chunk", 1 - RAW) * UNITS)
                    r = p.row0 + c * KT * P
                    sp.dma_start(raw[:, n % RAW],
                                 src[r:r + KT * P, bass.ds(p.col(i), PW)].rearrange("(t p) n -> p t n", p=P)
                                 ).then_inc(raw_landed[n % RAW], 16)
                    cnt.n["chunk"] += 1

            def loops():
                for st in stages:
                    if st.iters == 1:
                        body(st, 0)
                    else:
                        with sp.Fori(0, st.iters) as i:
                            cnt.i = i
                            start = cnt.n["chunk"]
                            cnt.per = {"chunk": sum(p.chunks for p in st.panels)}
                            body(st, i)
                        cnt.i = None
                        cnt.n["chunk"] = start + st.iters * cnt.per["chunk"]

            loops()
            for half in range(2):
                for m, scaled in ((0, scaled_dve), (1, scaled_act)):
                    cols = slice(half * (D // 2), (half + 1) * (D // 2))
                    sp.wait_ge(scaled, half + 1)
                    sp.dma_start(out[0, m * P:(m + 1) * P, cols], o_tok[:, m, cols]).then_inc(stored, 16)
            sp.wait_ge(stored, 64)

        def unit_of(n, u):
            return (n * UNITS + u) % SPLIT

        def landed_count(cnt, ahead):
            n = cnt.n["chunk"] + ahead
            base = 16 * (n // RAW + 1)
            if cnt.i is None:
                return base
            assert cnt.per["chunk"] % RAW == 0
            return cnt.i * (16 * cnt.per["chunk"] // RAW) + base

        @block.scalar
        def _(act):
            cnt = Counts()
            for v, r0 in ((norm_mix, V_MIX), (norm_mlp, V_MLP), (final_norm.rearrange("(a d) -> a d", a=1), V_FIN1),
                          (norm_mix_2.rearrange("(a d) -> a d", a=1), V_MIX2),
                          (norm_ffn_2.rearrange("(a d) -> a d", a=1), V_FFN2),
                          (norm_final_2.rearrange("(a d) -> a d", a=1), V_FIN2)):
                act.dma_start(gv[r0:r0 + NT, 0, :], v[0].rearrange("(t p) -> t p", p=P)).then_inc(vec_landed, 16)
            act.dma_start(gv[0:NT, 1, :], pool_scale.rearrange("(t p) -> t p", p=P)).then_inc(vec_landed, 16)
            act.dma_start(gv[NT:3 * NT, 1, :], b_gate.rearrange("(t p) -> t p", p=P)).then_inc(vec_landed, 16)
            act.dma_start(gv[3 * NT:6 * NT, 1, :], conv_w.rearrange("k (t p) -> (k t) p", p=P)).then_inc(vec_landed, 16)
            act.dma_start(meta_tok[:], meta).then_inc(meta_landed, 16)

            def split_hi(ahead=AHEAD // UNITS):
                n = cnt.n["chunk"] + ahead
                if n >= n_chunks:
                    return
                act.wait_ge(raw_landed[n % RAW], landed_count(cnt, ahead))
                for u in range(UNITS):
                    if cnt.i is not None or n * UNITS + u >= SPLIT:
                        act.wait_ge(w_used, cnt.at("chunk", ahead) * UNITS + (u + 1 - SPLIT))
                    act.activation(whi[:, unit_of(n, u)], raw[:, n % RAW, u * UK:(u + 1) * UK, :],
                                   ACT.Copy).then_inc(w_hi, 1)

            for j in range(CH):
                act.wait_ge(tr_done, j + 1)
                act.activation(tiles(h, j), x_bank(j), ACT.Copy).then_inc(act_done, 1)
                if j < AHEAD // UNITS:
                    split_hi(j)
                act.wait_ge(full_ready, cnt.at("full", 1))
                act.activation(tiles(a_hi, j, M), full[:], ACT.Copy).then_inc(act_done, 1)
                cnt.event("x")

            def token_squares(m):
                if m > 0:
                    act.wait_ge(ssq_ready, m)
                act.activation(x_sq[:], x_tok[:, m, :], ACT.Square, accum_out=stat[:, m:m + 1]).then_inc(ssq_ready, 1)

            def evac(kind, j):
                dst = {"q": tiles(b_hi, j), "k": k_hi[:], "v": v_hi[:], "res": tiles(a_hi, j, M),
                       "res2": tiles(a_hi, j, M), "up": tiles(a_hi, j, M), "relu2": tiles(b_hi, j), "co": tiles(a_hi, j, M), "resb": tiles(b_hi, j),
                       "gb": tiles(b_hi, j), "attn": tiles(b_hi, j)}
                if kind == "fin":
                    act.wait_ge(full_ready, cnt.at("full", 1))
                    act.activation(sqt, tiles(h, j), ACT.Square).then_inc(act_done, 1)
                    act.wait_ge(y_t, j + 1)
                    act.activation(o_tok[:, :, j * PW:(j + 1) * PW], ps[:, 2:4, :], ACT.Copy).then_inc(act_done, 1)
                    return
                if not KINDS[kind].get("act"):
                    return
                act.wait_ge(full_ready, cnt.at("full", 1))
                if kind == "ga":
                    act.activation(tiles(za, j), full[:], ACT.Sigmoid).then_inc(act_done, 1)
                elif kind == "gbr":
                    act.activation(tiles(G, j), full[:], ACT.Sigmoid).then_inc(act_done, 1)
                elif kind == "gate":
                    act.activation(S1[:, :, 0:T], U[:, :, 0:T], ACT.Sigmoid).then_inc(act_done, 1)
                else:
                    src = full[:].rearrange("p a b -> p (a b)").rearrange("p (a b) -> p a b", b=PW) if kind == "v" else full[:]
                    act.activation(dst[kind], src, ACT.Copy).then_inc(act_done, 1)
                if kind in ("res", "resb", "res2"):
                    act.wait_ge(sq_step, cnt.at("sq"))
                    if kind == "res2":
                        act.activation(U[:, :, 0:T], U[:, :, 0:T], ACT.Square).then_inc(act_done, 1)
                    act.activation(sqt, tiles(h, j), ACT.Square).then_inc(act_done, 1)

            def root(k):
                act.wait_ge(ms_ready, NORM_AT[k])
                act.activation(ms[:, 1, M:TW], ms[:, 0, M:TW], ACT.Sqrt).then_inc(root_ready, 1)
                if k == 1:
                    act.wait_ge(ms_ready, NORM_AT[k] + 1)
                    act.activation(ms[:, 1, :], ms[:, 0, :], ACT.Sqrt).then_inc(root_ready, 1)

            def weights_exp(g):
                act.wait_ge(arg_ready, g + 1)
                for b, hd in ((2, 0), (6, 2)):
                    last = act.activation(t1[:, hd:hd + 2, :], ps[:, b:b + 2, 0:3 * P], ACT.Exp)
                last.then_inc(a_exp, 1)

            def weights_hi(g):
                act.wait_ge(a_full, g + 1)
                act.activation(p_hi[:], t1[:], ACT.Copy).then_inc(aw_hi, 1)

            def softplus_ln(g):
                act.wait_ge(z_read, g + 1)
                act.activation(t1[:], t1[:], ACT.Exp).then_inc(act_chain, 1)
                act.wait_ge(act_chain, g + 1)
                act.activation(t1[:], t1[:], ACT.Ln, bias=1.0).then_inc(sp_ln, 1)

            def softplus_hi(g):
                act.wait_ge(sp_full, g + 1)
                act.activation(p_hi[:], t2[:], ACT.Copy).then_inc(sp_hi, 1)

            def body(st, i):
                for q, (k, c) in enumerate(st.order):
                    p = st.panels[k]
                    split_hi()
                    cnt.n["chunk"] += 1
                    if st.name == "q" and k == 0 and c < MT:
                        token_squares(c)
                        if c == MT - 1:
                            act.wait_ge(ms_ready, 1)
                            act.activation(stat[:, 4:6], stat[:, 2:4], ACT.Sqrt).then_inc(root_ready, 1)
                    if st.name == "q" and k == 1 and c == 0:
                        act.wait_ge(meta_step, 2)
                        act.activation(a_hi[:, :, 0:M], S1[:, 0, 0:NT * M].rearrange("p (t n) -> p t n", n=M),
                                       ACT.Copy).then_inc(meta_hi, 1)
                    if st.norm is not None and k == 0 and c == NORM_CHUNK:
                        root(st.norm)
                    if c == p.chunks - 1:
                        evac(p.kind, k // 2 if p.kind in ("k", "v") else st.index(i, k))
                        cnt.event(p.kind)
                    for g, step in attn_steps(st, q):
                        if step == 2:
                            softplus_ln(g)
                        if step == 4:
                            softplus_hi(g)
                        if step == 6:
                            weights_exp(g)
                        if step == 7:
                            weights_hi(g)
                        if step == 8:
                            evac("attn", g)
                            cnt.event("attn")

            run(act, cnt, body)
            act.wait_ge(ms_ready, NORM_AT[3])
            act.activation(stat[:, 4:6], stat[:, 2:4], ACT.Sqrt).then_inc(root_ready, 1)
            act.wait_ge(col_ready, 1)
            act.wait_ge(act_done, cnt.at("act"))
            for half in range(2):
                cols = slice(half * (D // 2), (half + 1) * (D // 2))
                act.activation(o_tok[:, 1, cols], o_tok[:, 1, cols], ACT.Copy,
                               scale=stat[:, 1:2]).then_inc(scaled_act, 1)

        @block.vector
        def _(dve):
            cnt = Counts()
            mid = [0]

            def step(ins):
                mid[0] += 1
                ins.then_inc(dve_mid, 1)
                dve.wait_ge(dve_mid, cnt.at("mid", mid[0]))

            def split_lo(ahead=AHEAD // UNITS):
                n = cnt.n["chunk"] + ahead
                if n >= n_chunks:
                    return
                dve.wait_ge(raw_landed[n % RAW], landed_count(cnt, ahead))
                for u in range(UNITS):
                    dve.wait_ge(w_hi, cnt.at("chunk", ahead) * UNITS + (u + 1))
                    s = unit_of(n, u)
                    dve.tensor_tensor(wlo[:, s], raw[:, n % RAW, u * UK:(u + 1) * UK, :], cast(whi[:, s]),
                                      ALU.subtract).then_inc(w_lo, 1)

            dve.memset(ones[:], 1.0)
            dve.memset(acc[:], 0.0).then_inc(consts, 1)
            dve.wait_ge(vec_t, 1)
            dve.tensor_copy(vec[:], ps[:, 5, 0:192]).then_inc(vec_ready, 1)
            dve.wait_ge(vec_ready, 1)
            for j in range(CH):
                dve.wait_ge(act_done, cnt.at("act", 1))
                if j > 0:
                    dve.wait_ge(pool_done, cnt.at("pool"))
                dve.tensor_tensor(full[:], tiles(h, j), gain(V_MIX, j), ALU.mult).then_inc(full_ready, 1)
                if j < AHEAD // UNITS:
                    split_lo(j)
                cnt.event("x")

            def token_rms():
                dve.wait_ge(ssq_ready, 2)
                dve.tensor_scalar(stat[:, 2:4], stat[:, 0:2], 1.0 / D, EPS, ALU.mult, ALU.add).then_inc(ms_ready, 1)
                dve.wait_ge(root_ready, 1)
                dve.reciprocal(stat[:, 6:8], stat[:, 4:6]).then_inc(rstd_ready, 1)
                dve.wait_ge(rstd_ready, 1)
                for m in range(MT):
                    last = dve.tensor_scalar(S2[:, m, 0:P], ident[:], stat[:, 6 + m:7 + m], None, ALU.mult)
                last.then_inc(diag_ready, 1)

            def token_rows():
                dve.wait_ge(rr_mm, 1)
                dve.tensor_copy(rr[:, M:TW], ps[:, 7, 0:T]).then_inc(diag_ready, 1)
                dve.wait_ge(diag_ready, 2)

            def meta_operand():
                meta_raw = U[:, 0, 0:NT * M]
                meta_f = S1[:, 0, 0:NT * M].rearrange("p (t n) -> p t n", n=M)
                dve.wait_ge(meta_t, 1)
                dve.tensor_copy(meta_raw, ps[:, 6, T:T + NT * M]).then_inc(meta_step, 1)
                dve.wait_ge(meta_step, 1)
                dve.tensor_tensor(meta_f, meta_raw.rearrange("p (t n) -> p t n", n=M),
                                  vec[:, V_MIX2:V_MIX2 + NT].unsqueeze(2).to_broadcast([P, NT, M]),
                                  ALU.mult).then_inc(meta_step, 1)
                dve.wait_ge(meta_step, 2)
                dve.tensor_tensor(U[:, 1, 0:NT * M], meta_raw, meta_raw, ALU.mult).then_inc(meta_step, 1)
                dve.wait_ge(meta_hi, 1)
                dve.tensor_tensor(a_lo[:, :, 0:M], meta_f, cast(a_hi[:, :, 0:M]), ALU.subtract).then_inc(meta_step, 1)
                dve.wait_ge(meta_step, 4)
                dve.tensor_reduce(msum[:], U[:, 1, 0:NT * M].rearrange("p (t n) -> p n t", n=M), mybir.AxisListType.X,
                                  ALU.add).then_inc(meta_step, 1)

            def z_out(g):
                dve.wait_ge(z_ready, g + 1)
                dve.wait_ge(meta_step, 5)
                if g > 0:
                    dve.wait_ge(aw_lo, g)
                for b, hd in ((2, 0), (6, 2)):
                    last = dve.tensor_scalar(t2[:, hd:hd + 2, :], ps[:, b:b + 2, 0:3 * P], 0.0, None, ALU.max)
                last.then_inc(z_mid, 1)
                dve.wait_ge(z_mid, g + 1)
                for b, hd in ((2, 0), (6, 2)):
                    last = dve.scalar_tensor_tensor(out=t1[:, hd:hd + 2, :], in0=t2[:, hd:hd + 2, :], scalar=-2.0,
                                                    in1=ps[:, b:b + 2, 0:3 * P], op0=ALU.mult, op1=ALU.add)
                last.then_inc(z_read, 1)

            def softplus_sum(g):
                dve.wait_ge(sp_ln, g + 1)
                dve.tensor_tensor(t2[:], t2[:], t1[:], ALU.add).then_inc(sp_raw, 1)

            def softplus_lo(g):
                dve.wait_ge(sp_hi, g + 1)
                dve.tensor_tensor(p_lo[:], t2[:], cast(p_hi[:]), ALU.subtract).then_inc(sp_lo, 1)

            def weights_lo(g):
                dve.wait_ge(aw_hi, g + 1)
                dve.tensor_tensor(p_lo[:], t1[:], cast(p_hi[:]), ALU.subtract).then_inc(aw_lo, 1)

            def attn_out(g):
                mid[0] = 0
                dve.wait_ge(o_ready, g + 1)
                dve.wait_ge(pool_done, cnt.at("pool"))
                dve.tensor_copy(full[:, 0:2, :], ps[:, 2:4, 0:T]).then_inc(dve_mid, 1)
                dve.tensor_copy(full[:, 2:4, :], ps[:, 6:8, 0:T]).then_inc(full_ready, 1)
                cnt.event("attn")

            def norm(k):
                dve.wait_ge(norm_mm, k + 1)
                dve.tensor_scalar(ms[:, 0, M:TW], ps[:, 7, 0:T], 1.0 / D, EPS, ALU.mult, ALU.add).then_inc(ms_ready, 1)
                dve.wait_ge(root_ready, NORM_AT[k])
                if k != 1:
                    dve.reciprocal(rr[:, M:TW], ms[:, 1, M:TW]).then_inc(rstd_ready, 1)
                else:
                    dve.reciprocal(rr1[:], ms[:, 1, M:TW]).then_inc(norm_mid, 1)
                    dve.wait_ge(norm_mid, 1)
                    dve.tensor_tensor(ms[:, 0, M:TW], ps[:, 6, M:TW], rr1[:], ALU.mult).then_inc(norm_mid, 1)
                    dve.wait_ge(norm_mid, 2)
                    dve.tensor_tensor(ms[:, 0, M:TW], ms[:, 0, M:TW], rr1[:], ALU.mult)
                    dve.tensor_copy(ms[:, 0, 0:M], ps[:, 6, 0:M]).then_inc(norm_mid, 1)
                    dve.wait_ge(norm_mid, 3)
                    dve.tensor_scalar(ms[:, 0, :], ms[:, 0, :], 1.0 / D, EPS, ALU.mult, ALU.add).then_inc(ms_ready, 1)
                    dve.wait_ge(root_ready, NORM_AT[k] + 1)
                    dve.reciprocal(rr[:], ms[:, 1, :]).then_inc(norm_mid, 1)
                    dve.wait_ge(norm_mid, 4)
                    dve.tensor_tensor(rr[:, M:TW], rr[:, M:TW], rr1[:], ALU.mult).then_inc(rstd_ready, 1)
                dve.wait_ge(rstd_ready, k + 2)

            def evac(kind, half, j):
                mid[0] = 0
                dve.wait_ge(w_used, cnt.at("chunk") * UNITS)
                dve.wait_ge(full_ready, cnt.at("full"))
                dve.wait_ge(act_done, cnt.at("act"))
                dve.wait_ge(pool_done, cnt.at("pool"))
                n = narrow(half)
                r = rows(rr[:, M:TW], T)
                if kind == "q":
                    last = dve.scalar_tensor_tensor(out=full[:], in0=n, scalar=QK_SCALE, in1=r,
                                                    op0=ALU.mult, op1=ALU.mult)
                elif kind == "k":
                    last = dve.tensor_tensor(full[:], n, r, ALU.mult)
                elif kind == "v":
                    for m in range(MT):
                        last = dve.tensor_scalar(full[:].rearrange("p (m t) n -> p m (t n)", m=MT)[:, m, :],
                                                 ps[:, 4 * half + m, :], stat[:, 6 + m:7 + m], None, ALU.mult)
                elif kind == "add":
                    last = dve.tensor_tensor(tiles(h, j), tiles(h, j), n, ALU.add)
                elif kind in ("res", "resb"):
                    step(dve.tensor_tensor(tiles(h, j), tiles(h, j), n, ALU.add))
                    last = dve.tensor_tensor(full[:], tiles(h, j), gain(V_MLP if kind == "res" else V_FFN2, j), ALU.mult)
                elif kind == "res2":
                    dve.wait_ge(sq_step, cnt.at("sq"))
                    step(dve.tensor_tensor(U[:, :, 0:T], tiles(h, j), n, ALU.add))
                    step(dve.tensor_tensor(tiles(h, j), U[:, :, 0:T], gain(V_FIN1, j), ALU.mult))
                    last = dve.tensor_tensor(full[:], tiles(h, j), gain(V_MIX2, j), ALU.mult)
                elif kind == "relu2":
                    step(dve.tensor_tensor(full[:], n, r, ALU.mult))
                    last = dve.scalar_tensor_tensor(out=full[:], in0=full[:], scalar=0.0, in1=full[:],
                                                    op0=ALU.max, op1=ALU.mult)
                elif kind in ("u0", "u1", "u2", "u3"):
                    step(dve.tensor_tensor(U[:], wide(half), rows(rr[:], TW), ALU.mult))
                    src, bufs, w, lo = U, [S1, S2], 1, 0
                    while w < WINDOWS[j]:
                        lo += w
                        dst = bufs[0]
                        step(dve.tensor_tensor(dst[:, :, lo:TW], src[:, :, lo:TW], src[:, :, lo - w:TW - w], ALU.add))
                        src, bufs, w = dst, bufs[::-1], 2 * w
                    last = dve.scalar_tensor_tensor(out=full[:], in0=src[:, :, M:TW], scalar=1.0 / w,
                                                    in1=U[:, :, M:TW], op0=ALU.mult, op1=ALU.subtract)
                elif kind in ("ga", "gbr"):
                    step(dve.tensor_tensor(full[:], n, r, ALU.mult))
                    if kind == "ga":
                        step(dve.tensor_tensor(tiles(h, j), tiles(h, j), rows(rr1[:], T), ALU.mult))
                    last = dve.tensor_tensor(full[:], full[:], gain(V_BG if kind == "ga" else V_BG + NT, j), ALU.add)
                elif kind == "pw":
                    step(dve.tensor_tensor(full[:], n, gain(V_PS, j), ALU.mult))
                    last = dve.tensor_tensor(tiles(za, j), tiles(za, j), full[:], ALU.mult)
                elif kind == "gc":
                    last = dve.tensor_tensor(tiles(G, j, 0, TW), wide(half), rows(rr[:], TW), ALU.mult)
                elif kind == "vv":
                    step(dve.tensor_tensor(U[:], wide(half), rows(rr[:], TW), ALU.mult))
                    last = dve.tensor_tensor(U[:], U[:], tiles(G, j, 0, TW), ALU.mult)
                elif kind == "gb":
                    step(dve.tensor_tensor(full[:], n, r, ALU.mult))
                    last = dve.tensor_tensor(full[:], full[:], tiles(G, j), ALU.mult)
                elif kind == "co":
                    step(dve.tensor_tensor(full[:], n, tiles(G, j), ALU.mult))
                    last = dve.tensor_tensor(full[:], full[:], tiles(za, j), ALU.add)
                elif kind == "gate":
                    last = dve.tensor_tensor(U[:, :, 0:T], n, r, ALU.mult)
                elif kind == "up":
                    step(dve.tensor_tensor(full[:], n, r, ALU.mult))
                    last = dve.tensor_tensor(full[:], full[:], S1[:, :, 0:T], ALU.mult)
                elif kind == "fin":
                    step(dve.tensor_tensor(tiles(h, j), tiles(h, j), n, ALU.add))
                    if j > 0:
                        dve.wait_ge(y_t, j)
                    last = dve.tensor_tensor(full[:], tiles(h, j), gain(V_FIN2, j), ALU.mult)
                last.then_inc(full_ready, 1)

            def body(st, i):
                for q, (k, c) in enumerate(st.order):
                    p = st.panels[k]
                    split_lo()
                    cnt.n["chunk"] += 1
                    if st.name == "q" and k == 0 and c == 1:
                        token_rms()
                    if st.name == "q" and k == 0 and c == 3:
                        token_rows()
                    if st.name == "q" and k == 1 and c == 0:
                        meta_operand()
                    if st.norm is not None and k == 0 and c == NORM_CHUNK:
                        norm(st.norm)
                    if c == p.chunks - 1:
                        evac(p.kind, k % 2, k // 2 if p.kind in ("k", "v") else st.index(i, k))
                        cnt.event(p.kind)
                    for g, s in attn_steps(st, q):
                        if s == 1:
                            z_out(g)
                        if s == 3:
                            softplus_sum(g)
                        if s == 5:
                            softplus_lo(g)
                        if s == 7:
                            weights_lo(g)
                        if s == 8:
                            attn_out(g)

            run(dve, cnt, body)
            dve.wait_ge(y_t, 4)
            dve.tensor_scalar(stat[:, 2:4], ps[:, 7, 0:4].rearrange("p (m n) -> p m n", n=2)[:, :, 0], 1.0 / D, EPS,
                              ALU.mult, ALU.add).then_inc(ms_ready, 1)
            dve.wait_ge(root_ready, NORM_AT[3])
            dve.reciprocal(stat[:, 0:2], stat[:, 4:6]).then_inc(col_ready, 1)
            dve.wait_ge(col_ready, 1)
            dve.wait_ge(act_done, cnt.at("act"))
            for half in range(2):
                cols = slice(half * (D // 2), (half + 1) * (D // 2))
                dve.tensor_scalar(o_tok[:, 0, cols], o_tok[:, 0, cols], stat[:, 0:1], None,
                                  ALU.mult).then_inc(scaled_dve, 1)

        @block.gpsimd
        def _(pool):
            cnt = Counts()
            pool.memset(ident[:], 0.0).then_inc(tri_ready, 1)
            pool.wait_ge(tri_ready, 1)
            pool.affine_select(out=ident[:], in_=ident[:], compare_op=ALU.not_equal, fill=1.0, base=0,
                               pattern=[[-1, P]], channel_multiplier=1).then_inc(consts, 1)
            pool.memset(tri32[:], -1.0).then_inc(tri_ready, 1)
            pool.wait_ge(tri_ready, 2)
            pool.tensor_copy(negone[:], tri32[:]).then_inc(tri_ready, 1)
            pool.wait_ge(tri_ready, 3)
            pool.affine_select(out=tri32[:], in_=tri32[:], compare_op=ALU.is_ge, fill=0.0, base=0,
                               pattern=[[-1, P]], channel_multiplier=1).then_inc(tri_ready, 1)
            pool.wait_ge(tri_ready, 4)
            pool.tensor_copy(negtri[:], tri32[:]).then_inc(tri_ready, 1)
            for j in range(CH):
                pool.wait_ge(act_done, cnt.at("act", 2))
                pool.tensor_tensor(tiles(a_lo, j, M), full[:], cast(tiles(a_hi, j, M)),
                                   ALU.subtract).then_inc(pool_done, 1)
                cnt.event("x")

            def lo_part(kind, j):
                to_b = ("q", "relu2", "gb", "attn", "resb", "u0", "u1", "u2", "u3")
                if kind == "k":
                    lo, hi, src = k_lo[:], k_hi[:], full[:]
                elif kind == "v":
                    lo, hi = v_lo[:], v_hi[:]
                    src = full[:].rearrange("p a b -> p (a b)").rearrange("p (a b) -> p a b", b=PW)
                elif kind in to_b:
                    lo, hi, src = tiles(b_lo, j), tiles(b_hi, j), full[:]
                else:
                    lo, hi, src = tiles(a_lo, j, M), tiles(a_hi, j, M), full[:]
                if kind in ("u0", "u1", "u2", "u3"):
                    pool.wait_ge(full_ready, cnt.at("full", 1))
                    pool.tensor_copy(hi, src).then_inc(pool_done, 1)
                    pool.wait_ge(pool_done, cnt.at("pool", 1))
                else:
                    pool.wait_ge(act_done, cnt.at("act", 1))
                pool.tensor_tensor(lo, src, cast(hi), ALU.subtract).then_inc(pool_done, 1)

            def add_squares(dst, sq, n):
                pool.wait_ge(act_done, cnt.at("act", 1 + n))
                pool.tensor_tensor(dst, dst, sq, ALU.add).then_inc(sq_step, 1)

            def conv(j):
                y, t = S1[:, :, 0:T], S2[:, :, 0:T]
                pool.wait_ge(full_ready, cnt.at("full", 1))
                for tap in range(3):
                    dst = y if tap == 0 else t
                    pool.tensor_tensor(dst, U[:, :, M - 2 + tap:TW - 2 + tap], gain(V_CV + tap * NT, j),
                                       ALU.mult).then_inc(pool_done, 1)
                    pool.wait_ge(pool_done, cnt.at("pool", 2 * tap if tap else 1))
                    if tap > 0:
                        pool.tensor_tensor(tiles(G, j) if tap == 2 else y, y, t, ALU.add).then_inc(pool_done, 1)
                        pool.wait_ge(pool_done, cnt.at("pool", 2 * tap + 1))

            def mask(t, before, after, g):
                pool.wait_ge(before, g + 1)
                for hd in range(GH):
                    v = t[:, hd, :].rearrange("p (b n) -> p b n", n=P)[:, 0:3:2, :]
                    last = pool.affine_select(out=v, in_=v, compare_op=ALU.is_gt, fill=0.0, base=0,
                                              pattern=[[0, 2], [1, P]], channel_multiplier=-1)
                last.then_inc(after, 1)

            def evac(kind, j):
                if kind == "gate":
                    pool.wait_ge(act_done, cnt.at("act", 1))
                    pool.tensor_tensor(S1[:, :, 0:T], S1[:, :, 0:T], U[:, :, 0:T], ALU.mult).then_inc(pool_done, 1)
                elif kind == "vv":
                    conv(j)
                elif KINDS[kind].get("pool"):
                    lo_part(kind, j)
                if kind in ("res", "resb"):
                    add_squares(acc[:], sqt, 1)
                if kind == "res2":
                    add_squares(acc[:], U[:, :, 0:T], 1)
                    add_squares(acc2, sqt, 2)

            def body(st, i):
                for q, (k, c) in enumerate(st.order):
                    p = st.panels[k]
                    cnt.n["chunk"] += 1
                    if c == p.chunks - 1:
                        evac(p.kind, k // 2 if p.kind in ("k", "v") else st.index(i, k))
                        cnt.event(p.kind)
                    for g, s in attn_steps(st, q):
                        if s == 4:
                            mask(t2, sp_raw, sp_full, g)
                        if s == 6:
                            mask(t1, a_exp, a_full, g)
                        if s == 8:
                            lo_part("attn", g)
                            cnt.event("attn")

            def fresh_sums(norms):
                pool.wait_ge(norm_mm, norms)
                if norms == 1:
                    pool.memset(acc2, 0.0)
                pool.memset(acc[:], 0.0).then_inc(tri_ready, 1)
                pool.wait_ge(tri_ready, 5 + norms)

            pool.wait_ge(consts, 2)
            for st in stages:
                if st.name in ("w2_3", "wo2"):
                    fresh_sums({"w2_3": 1, "wo2": 2}[st.name])
                if st.iters == 1:
                    body(st, 0)
                else:
                    with pool.Fori(0, st.iters) as i:
                        cnt.enter(st, i)
                        body(st, i)
                    cnt.leave(st)

        @block.tensor
        def _(pe):
            cnt = Counts()
            pe.wait_ge(consts, 2)
            for j in range(CH):
                pe.wait_ge(x_landed[j], 16)
                if j >= 2:
                    pe.wait_ge(act_done, KINDS["x"]["act"] * (j - 2) + 1)
                for t in range(JT):
                    for m in range(MT):
                        last = pe.transpose(x_bank(j)[:, t, m * P:(m + 1) * P],
                                            x_tok[:, m, (j * JT + t) * P:(j * JT + t + 1) * P], ident[:])
                last.then_inc(tr_done, 1)
                if j == 0:
                    pe.wait_ge(vec_landed, 16 * 9)
                    for b in range(2):
                        last = pe.transpose(ps[:, 5, 96 * b:96 * b + 96], gv[:, b, :], ident[0:96, 0:96])
                    last.then_inc(vec_t, 1)
                cnt.event("x")

            def meta_turn():
                pe.wait_ge(meta_landed, 16)
                pe.wait_ge(act_done, KINDS["x"]["act"] * 3 + 1)
                for t in range(NT):
                    last = pe.transpose(ps[:, 6, T + t * M:T + (t + 1) * M], meta_tok[:, t * P:(t + 1) * P],
                                        ident[0:M, 0:M])
                last.then_inc(meta_t, 1)

            def token_rows():
                pe.wait_ge(diag_ready, 1)
                for m in range(MT):
                    last = pe.matmul(ps[:, 7, m * P:(m + 1) * P], ones[:], S2[:, m, 0:P], start=(m == 0),
                                     stop=(m == MT - 1), skip_group_check=True)
                last.then_inc(rr_mm, 1)

            bufs = {"A": (a_hi, a_lo, M), "B": (b_hi, b_lo, 0)}

            def three(out, w_h, w_l, x_h, x_l, start, stop):
                pe.matmul(out, w_h, x_h, start=start, stop=False, skip_group_check=True)
                pe.matmul(out, w_h, x_l, start=False, stop=False, skip_group_check=True)
                return pe.matmul(out, w_l, x_h, start=False, stop=stop, skip_group_check=True)

            def chunk(p, c, half):
                n = cnt.n["chunk"]
                if p.needs:
                    pe.wait_ge(pool_done, ready[p.needs][c if p.chunks > 1 else p.tile0 // JT])
                hi, lo, off = bufs[p.src]
                for u in range(UNITS):
                    s = unit_of(n, u)
                    pe.wait_ge(w_lo, cnt.at("chunk") * UNITS + (u + 1))
                    for j in range(JT):
                        for kt in range(UK):
                            x = p.tile0 + c * KT + u * UK + kt
                            first = c == 0 and u == 0 and kt == 0
                            stop = c == p.chunks - 1 and u == UNITS - 1 and kt == UK - 1
                            if p.kind == "v":
                                if j >= MT:
                                    break
                                tok = slice(off + j * P, off + (j + 1) * P)
                                last = three(ps[:, 4 * half + j, :], hi[:, x, tok], lo[:, x, tok],
                                             whi[:, s, kt, :], wlo[:, s, kt, :], first, stop)
                                continue
                            cols = slice(j * P, (j + 1) * P)
                            if p.kind in WIDE:
                                o, tok = ps[:, 4 * half + j, 0:TW], slice(0, TW)
                            else:
                                o, tok = ps[:, 4 * half + j // 2, (j % 2) * T:(j % 2 + 1) * T], slice(off, off + T)
                                first = first and j % 2 == 0
                            last = three(o, whi[:, s, kt, cols], wlo[:, s, kt, cols], hi[:, x, tok], lo[:, x, tok],
                                         first, stop)
                    last.then_inc(w_used, 1)
                cnt.n["chunk"] += 1

            hb = (2, 3, 6, 7)

            def scores(g):
                pe.wait_ge(pool_done, cnt.at("pool", -1 if g > 0 else 0))
                if g > 0:
                    pe.wait_ge(full_ready, cnt.at("full"))
                for hd in range(GH):
                    t = g * GH + hd
                    three(ps[:, hb[hd], 0:T], k_hi[:, hd, 0:P], k_lo[:, hd, 0:P], b_hi[:, t, :], b_lo[:, t, :],
                          True, False)
                    last = three(ps[:, hb[hd], T:T + P], k_hi[:, hd, P:T], k_lo[:, hd, P:T],
                                 b_hi[:, t, P:T], b_lo[:, t, P:T], False, False)
                last.then_inc(z_ready, 1)

            def suffix_sums(g):
                pe.wait_ge(sp_lo, g + 1)
                pe.wait_ge(tri_ready, 5)
                for hd in range(GH):
                    for part in (p_hi, p_lo):
                        pe.matmul(ps[:, hb[hd], 0:T], negtri[:], part[:, hd, 0:T], start=False, stop=False,
                                  skip_group_check=True)
                        pe.matmul(ps[:, hb[hd], P:T], negone[:], part[:, hd, T:T + P], start=False, stop=False,
                                  skip_group_check=True)
                        last = pe.matmul(ps[:, hb[hd], T:T + P], negtri[:], part[:, hd, T:T + P], start=False,
                                         stop=part is p_lo, skip_group_check=True)
                last.then_inc(arg_ready, 1)

            def values(g):
                pe.wait_ge(aw_lo, g + 1)
                for hd in range(GH):
                    col = slice(hd * HD, (hd + 1) * HD)
                    three(ps[:, hb[hd], 0:T], v_hi[:, 0, col], v_lo[:, 0, col], p_hi[:, hd, 0:T], p_lo[:, hd, 0:T],
                          True, False)
                    last = three(ps[:, hb[hd], P:T], v_hi[:, 1, col], v_lo[:, 1, col], p_hi[:, hd, T:T + P],
                                 p_lo[:, hd, T:T + P], False, True)
                last.then_inc(o_ready, 1)

            def norm(k):
                pe.wait_ge(sq_step, cnt.n["sq"])
                for s in range(JT):
                    last = pe.matmul(ps[:, 7, 0:T], ones[:], acc[:, s, :], start=(s == 0), stop=(s == JT - 1),
                                     skip_group_check=True)
                if k == 1:
                    pe.wait_ge(meta_step, 5)
                    pe.matmul(ps[:, 6, 0:M], ones[:], msum[:], start=True, stop=True, skip_group_check=True)
                    for s in range(JT):
                        last = pe.matmul(ps[:, 6, M:TW], ones[:], acc2[:, s, :], start=False, stop=(s == JT - 1),
                                         skip_group_check=True)
                last.then_inc(norm_mm, 1)

            def turn(j):
                pe.wait_ge(full_ready, cnt.at("full"))
                pe.wait_ge(act_done, cnt.at("act", -1))
                for m in range(MT):
                    for t in range(JT):
                        last = pe.transpose(ps[:, 2 + m, t * P:(t + 1) * P], full[:, t, m * P:(m + 1) * P], ident[:])
                for m in range(MT):
                    for t in range(JT):
                        last = pe.matmul(ps[:, 7, 2 * m:2 * m + 2], S2[:, t, m * P:(m + 1) * P], ones[:, 0:2],
                                         start=(j == 0 and m == 0 and t == 0), stop=(j == 3 and t == JT - 1),
                                         skip_group_check=True)
                last.then_inc(y_t, 1)

            def banks_free(st, k):
                back = -1
                if st.name == "q" and k < 2:
                    back = 0
                if st.name == "kv" and k >= 2 and k % 2 == 0 or st.name == "w_o" and k == 0:
                    back = -2
                if st.name == "w_o" and k == 1:
                    back = 0
                pe.wait_ge(full_ready, cnt.at("full", back))

            def body(st, i):
                for q, (k, c) in enumerate(st.order):
                    p = st.panels[k]
                    if c == 0:
                        banks_free(st, k)
                        if st.name == "q" and k == 1:
                            pe.wait_ge(vec_ready, 1)
                        if st.name == "u" and k == 0:
                            pe.wait_ge(meta_step, 5)
                        if st.name == "u" and k == 1:
                            pe.wait_ge(rstd_ready, 3)
                    chunk(p, c, k % 2)
                    if st.name == "q" and k == 0 and c == 1:
                        meta_turn()
                    if st.name == "q" and k == 0 and c == 2:
                        token_rows()
                    if c == 0 and st.name == "dn_2" and k > 0:
                        turn(k - 1)
                    if st.norm is not None and k == 0 and c == NORM_CHUNK:
                        norm(st.norm)
                    if c == p.chunks - 1:
                        cnt.event(p.kind)
                    for g, s in attn_steps(st, q):
                        if s == 1:
                            scores(g)
                        if s == 6:
                            suffix_sums(g)
                        if s == 8:
                            values(g)
                            cnt.event("attn")

            run(pe, cnt, body)
            turn(3)


_INS = ["x", "meta_tokens_2", "norm_mix", "norm_mlp", "final_norm", "sb_w_qkv", "sb_w_o", "mlp_w1", "mlp_w2",
        "norm_mix_g_2", "w_in_2", "b_gate_2", "pool_w_2", "pool_scale_2", "conv_w_2", "conv_out_w_2", "w_o_2",
        "norm_ffn_g_2", "w_gate_up_2", "w_down_2", "norm_final_g_2"]


def kernel(**inputs):
    import numpy as np
    import concourse.bacc as bacc
    from concourse.bass_utils import run_bass_kernel_spmd

    nc = bacc.Bacc("TRN2", target_bir_lowering=False, num_devices=1)
    arrays, args = {}, []
    for name in _INS:
        a = np.ascontiguousarray(inputs[name])
        arrays[f"in_{name}_dram"] = a
        args.append(nc.dram_tensor(f"in_{name}_dram", a.shape, mybir.dt.from_np(a.dtype), kind="ExternalInput").ap())
    out = nc.dram_tensor("out_dram", (1, T, D), F32, kind="ExternalOutput").ap()
    build(nc, *args, out)
    r = run_bass_kernel_spmd(nc, [arrays], core_ids=[0])
    return r.results[0]["out_dram"]
```

```python
from contextlib import ExitStack

import concourse.bass as bass
from concourse import mybir

ALU = mybir.AluOpType
ACT = mybir.ActivationFunctionType
F32 = mybir.dt.float32
F32R = mybir.dt.float32r

P = 128
D = 2048
NT = D // P
T = 256
MT = T // P
M = 16
TW = M + T
HD = 128
HEADS = D // HD
GH = 4
KT = 4
PW = 512
JT = PW // P
CH = D // (KT * P)
D_FF = 4 * D
FFN = 5632
WINDOWS = (2, 4, 8, 16)
EPS = 1e-6
QK_SCALE = HD ** -0.5
RAW = 4
UK = 2
UNITS = KT // UK
SPLIT = 4
AHEAD = SPLIT

KINDS = {
    "x": dict(full=1, act=2, pool=1),
    "q": dict(full=1, act=1, pool=1),
    "k": dict(full=1, act=1, pool=1),
    "v": dict(full=1, act=1, pool=1),
    "attn": dict(full=1, act=1, pool=1, mid=1),
    "res": dict(full=1, act=2, pool=1, mid=1, sq=1),
    "resb": dict(full=1, act=3, pool=1, mid=2, sq=1),
    "res2": dict(full=1, act=3, pool=1, mid=3, sq=3),
    "add": dict(full=1, act=1, mid=1),
    "relu2": dict(full=1, act=2, pool=1, mid=2),
    "u0": dict(full=1, pool=2, mid=2),
    "u1": dict(full=1, pool=2, mid=3),
    "u2": dict(full=1, pool=2, mid=4),
    "u3": dict(full=1, pool=2, mid=5),
    "ga": dict(full=1, act=2, mid=2, pool=2),
    "pw": dict(full=1),
    "gc": dict(full=1),
    "vv": dict(full=1, pool=5, mid=1),
    "gb": dict(full=1, act=2, pool=1, mid=2),
    "gbr": dict(full=1, act=2, mid=2),
    "co": dict(full=1, act=2, pool=1, mid=2),
    "gate": dict(full=1, act=2, pool=1, mid=1),
    "up": dict(full=1, act=2, pool=1, mid=2),
    "fin": dict(full=1, act=2, mid=4),
}
PAIRED = ("add", "relu2", "res2", "resb", "ga", "gb", "gbr", "co", "gate", "up")
WIDE = dict([(f"u{g}", (M + 1 - w) // 2 * 2) for g, w in enumerate(WINDOWS)] + [("gc", M - 2), ("vv", M - 2)])
NORM_AT = (2, 3, 5, 6)
NORM_CHUNK = 2
NAMES = ("chunk", "full", "act", "pool", "mid", "sq")


class Panel:

    def __init__(self, kind, weight, row0, col, chunks=CH, tile0=0, src=None, needs=None):
        self.kind, self.weight, self.row0, self.col = kind, weight, row0, col
        self.chunks, self.tile0, self.src, self.needs = chunks, tile0, src, needs


class Stage:

    def __init__(self, name, iters, panels, index=None, norm=None, order=None, attn=None):
        self.name, self.iters, self.panels, self.norm = name, iters, panels, norm
        self.order = order or [(k, c) for k, p in enumerate(panels) for c in range(p.chunks)]
        self.attn = attn
        self.index = index or (lambda i, k: i * len(panels) + k)


def attn_steps(st, q):
    if st.attn is None:
        return []
    steps = [(g, st.attn + q - (8 * g + 4)) for g in range(HEADS // GH)]
    return [(g, s) for g, s in steps if 0 <= s <= 8]


def attn_over(st, q):
    return st.attn is None or st.attn + q - (8 * (HEADS // GH - 1) + 4) > 8


class Counts:

    def __init__(self):
        self.n = {k: 0 for k in NAMES}
        self.i, self.per = None, None

    def at(self, name, more=0):
        v = self.n[name] + more
        return v if self.i is None else self.i * self.per[name] + v

    def enter(self, stage, i):
        self.i = i
        self.start = dict(self.n)
        self.per = {k: 0 for k in NAMES}
        for p in stage.panels:
            self.per["chunk"] += p.chunks
            for k, v in KINDS[p.kind].items():
                self.per[k] += v

    def leave(self, stage):
        self.i = None
        for k in NAMES:
            assert self.n[k] == self.start[k] + self.per[k], (stage.name, k)
            self.n[k] = self.start[k] + stage.iters * self.per[k]

    def event(self, kind):
        for k, v in KINDS[kind].items():
            self.n[k] += v


def make_stages():
    stages = []
    c = Counts()
    ready = {}

    def add(name, iters, panels, makes=None, norm=None, index=None):
        assert norm is None or iters == 1
        stages.append(Stage(name, iters, panels, index, norm))
        made = []
        for i in range(iters):
            for p in panels:
                c.n["chunk"] += p.chunks
                c.event(p.kind)
                if makes and p.kind in makes:
                    made.append(c.n["pool"])
        ready[name] = made
        return made

    for _ in range(CH):
        c.event("x")
    ready["x"] = [c.n["pool"] - CH + 1 + j for j in range(CH)]
    add("q", 1, [Panel("q", "w_qkv", 0, lambda i, g=g: g * PW, src="A", needs="x") for g in range(4)], ("q",))
    kv = []
    o_ready = []
    for g in range(4):
        kv.append(Panel("k", "w_qkv", 0, lambda i, g=g: D + g * PW, src="A"))
        kv.append(Panel("v", "w_qkv", 0, lambda i, g=g: 2 * D + g * PW, src="A"))
    stages.append(Stage("kv", 1, kv, attn=0))
    for kind in ("k", "v", "k", "attn", "v", "k", "attn", "v", "k", "attn", "v", "attn"):
        c.event(kind)
        if kind == "attn":
            o_ready.append(c.n["pool"])
    c.n["chunk"] += len(kv) * CH
    ready["kv"] = o_ready
    add("w_o", 1, [Panel("res", "w_o1", 0, lambda i, g=g: g * PW, src="B", needs="kv") for g in range(4)], ("res",))
    stages[-1].order = ([(0, 0), (0, 1), (0, 2), (1, 0), (1, 1), (1, 2), (0, 3), (1, 3)] +
                        [(k, ch) for k in (2, 3) for ch in range(CH)])
    stages[-1].attn = len(kv) * CH
    for f in range(D_FF // D):
        if f == 0:
            add("w1_0", 1, [Panel("relu2", "w1", 0, lambda i, g=g: g * PW, src="A", needs="w_o") for g in range(4)],
                ("relu2",), norm=0)
        else:
            add(f"w1_{f}", 2, [Panel("relu2", "w1", 0, lambda i, f=f, h=h: f * D + i * 2 * PW + h * PW, src="A",
                                     needs="w_o") for h in range(2)], ("relu2",))
        kind = "res2" if f == D_FF // D - 1 else "add"
        add(f"w2_{f}", 2, [Panel(kind, "w2", f * D, lambda i, h=h: i * 2 * PW + h * PW, src="B", needs=f"w1_{f}")
                           for h in range(2)], (kind,))
    add("u", 1, [Panel(f"u{g}", "w_in", 0, lambda i, g=g: g * PW, src="A", needs="w2_3") for g in range(4)],
        ("u0", "u1", "u2", "u3"), norm=1)

    def loop2(name, kind, weight, col0, src, needs=None, **kw):
        add(name, 2, [Panel(kind, weight, 0, lambda i, h=h: col0 + i * 2 * PW + h * PW, src=src, needs=needs)
                      for h in range(2)], (kind,), **kw)

    loop2("ga", "ga", "w_in", 4 * D, "A")
    add("pw", 1, [Panel("pw", "pool_w", g * PW, lambda i: 0, chunks=1, tile0=g * JT, src="B", needs="u")
                  for g in range(4)])
    loop2("gc", "gc", "w_in", 2 * D, "A")
    loop2("vv", "vv", "w_in", 3 * D, "A")
    loop2("gb", "gb", "w_in", 1 * D, "A")
    loop2("gbr", "gbr", "w_in", 5 * D, "A")
    loop2("co", "co", "conv_out_w", 0, "B", "gb")
    loop2("wo2", "resb", "w_o2", 0, "A", "co")

    def gate_up(name, d, n, j0=0, norm=None):
        return add(name, n, [Panel("gate", "w_gate_up", 0, lambda i: (d + i) * PW, src="B", needs="wo2"),
                             Panel("up", "w_gate_up", 0, lambda i: FFN + (d + i) * PW, src="B", needs="wo2")],
                   ("up",), norm=norm, index=lambda i, k: i + j0)

    done = 0
    for f, n in enumerate((4, 4, 3)):
        if f == 0:
            ready["gu_0"] = gate_up("gu_first", 0, 1, norm=2) + gate_up("gu_rest", 1, n - 1, j0=1)
        else:
            gate_up(f"gu_{f}", done, n)
        if n == 4:
            add(f"dn_{f}", 2, [Panel("add", "w_down", done * PW, lambda i, h=h: i * 2 * PW + h * PW, src="A",
                                     needs=f"gu_{f}") for h in range(2)])
        else:
            add(f"dn_{f}", 1, [Panel("fin", "w_down", done * PW, lambda i, g=g: g * PW, chunks=n, src="A",
                                     needs=f"gu_{f}") for g in range(4)])
        done += n
    return stages, ready, c.n["chunk"]


def build(nc, x, meta, norm_mix, norm_mlp, final_norm, w_qkv, w_o1, w1, w2, norm_mix_2, w_in, b_gate,
          pool_w, pool_scale, conv_w, conv_out_w, w_o2, norm_ffn_2, w_gate_up, w_down, norm_final_2, out):
    stages, ready, n_chunks = make_stages()
    dram = dict(w_qkv=w_qkv[0], w_o1=w_o1[0], w1=w1[0], w2=w2[0], w_in=w_in,
                pool_w=pool_w.rearrange("g c n -> (g c) n"), conv_out_w=conv_out_w, w_o2=w_o2,
                w_gate_up=w_gate_up, w_down=w_down)

    with ExitStack() as ctx:
        top = [(nc.sbuf_base + 63) // 64 * 64]
        arena_bytes = 0

        def place(name, shape, dt=F32, at=None):
            size = 4
            for s in shape[1:]:
                size *= s
            size = (size + 31) // 32 * 32
            off = top[0] if at is None else at
            if at is None:
                top[0] += size
            return nc.alloc_sbuf_tensor_at(name, shape, dt, offset=off), off

        def sem(name):
            return ctx.enter_context(nc.semaphore(name))

        raw, _ = place("raw", [P, RAW, KT, PW])
        whi, _ = place("whi", [P, SPLIT, UK, PW], F32R)
        wlo, _ = place("wlo", [P, SPLIT, UK, PW], F32R)
        a_buf, _ = place("a_buf", [P, 2, NT, TW], F32R)
        b_buf, b_off = place("b_buf", [P, 2, NT, T], F32R)
        a_hi, a_lo, b_hi, b_lo = a_buf[:, 0], a_buf[:, 1], b_buf[:, 0], b_buf[:, 1]
        h, _ = place("h", [P, NT, T])
        full, _ = place("full", [P, JT, T])
        U, u_off = place("U", [P, JT, TW])
        S1, s1_off = place("S1", [P, JT, TW])
        S2, s2_off = place("S2", [P, JT, TW])
        acc, _ = place("acc", [P, JT, T])
        rr, _ = place("rr", [P, TW])
        rr1, _ = place("rr1", [P, T])
        ms, _ = place("ms", [P, 2, TW])
        msum, _ = place("msum", [P, M])
        vec, _ = place("vec", [P, 192])
        ident, _ = place("ident", [P, P])
        ones, _ = place("ones", [P, P])
        negtri, _ = place("negtri", [P, P], F32R)
        negone, _ = place("negone", [P, P], F32R)
        stat, _ = place("stat", [P, 8])
        region = top[0]
        za, _ = place("za", [P, NT, T])
        G, _ = place("G", [P, NT, TW])
        at = region
        k_hi, _ = place("k_hi", [P, JT, T], F32R, at=at)
        k_lo, _ = place("k_lo", [P, JT, T], F32R, at=at + 4096)
        v_hi, _ = place("v_hi", [P, MT, PW], F32R, at=at + 8192)
        v_lo, _ = place("v_lo", [P, MT, PW], F32R, at=at + 12288)
        t1, _ = place("t1", [P, GH, 3 * P], at=at + 16384)
        p_hi, _ = place("p_hi", [P, GH, 3 * P], F32R, at=at + 22528)
        t2, _ = place("t2", [P, GH, 3 * P], at=u_off)
        p_lo, p_off = place("p_lo", [P, GH, 3 * P], F32R, at=at + 28672)
        top[0] = max(top[0], p_off + 4 * GH * 3 * P)
        acc2 = S1[:, :, 0:T]
        sqt = S2[:, :, 0:T]
        x_tok, _ = place("x_tok", [P, MT, D], at=region)
        meta_tok, _ = place("meta_tok", [M, D], at=region + 16384)
        x_sq, _ = place("x_sq", [P, MT, D], at=b_off)
        gm, _ = place("gm", [NT, P], at=region + 24576 + 1536)
        gv, _ = place("gv", [96, 2, P], at=region + 24576)
        tri32, _ = place("tri32", [P, P], at=region + 24576 + 1024)
        o_tok, _ = place("o_tok", [P, MT, D], at=region)
        arena_bytes = top[0] - nc.sbuf_base
        ctx.enter_context(nc.sbuf_tensor("arena", [P, arena_bytes // 4], F32))

        ps = ctx.enter_context(nc.psum_tensor("ps", [P, 8, 512], F32))

        V_MIX, V_MLP, V_FIN1, V_MIX2, V_FFN2, V_FIN2 = (NT * i for i in range(6))
        V_PS, V_BG, V_CV = 96, 96 + NT, 96 + 3 * NT

        raw_landed = [sem(f"raw_landed{s}") for s in range(RAW)]
        w_hi = sem("w_hi")
        w_lo = sem("w_lo")
        w_used = sem("w_used")
        full_ready = sem("full_ready")
        act_done = sem("act_done")
        pool_done = sem("pool_done")
        dve_mid = sem("dve_mid")
        sq_step = sem("sq_step")
        x_landed = [sem(f"x_landed{j}") for j in range(CH)]
        mix_landed = sem("mix_landed")
        vec_landed = sem("vec_landed")
        meta_landed = sem("meta_landed")
        consts = sem("consts")
        tri_ready = sem("tri_ready")
        ssq_ready = sem("ssq_ready")
        ms_ready = sem("ms_ready")
        root_ready = sem("root_ready")
        rstd_ready = sem("rstd_ready")
        diag_ready = sem("diag_ready")
        rr_mm = sem("rr_mm")
        vec_t = sem("vec_t")
        vec_ready = sem("vec_ready")
        tr_done = sem("tr_done")
        meta_t = sem("meta_t")
        meta_step = sem("meta_step")
        meta_hi = sem("meta_hi")
        norm_mm = sem("norm_mm")
        norm_mid = sem("norm_mid")
        h_scaled = sem("h_scaled")
        z_ready = sem("z_ready")
        z_mid = sem("z_mid")
        z_read = sem("z_read")
        sp_ln = sem("sp_ln")
        sp_raw = sem("sp_raw")
        sp_full = sem("sp_full")
        sp_hi = sem("sp_hi")
        sp_lo = sem("sp_lo")
        arg_ready = sem("arg_ready")
        a_exp = sem("a_exp")
        act_chain = sem("act_chain")
        a_full = sem("a_full")
        aw_hi = sem("aw_hi")
        aw_lo = sem("aw_lo")
        o_ready = sem("o_ready")
        gate_s = sem("gate_s")
        y_t = sem("y_t")
        y_sums = sem("y_sums")
        col_ready = sem("col_ready")
        scaled_dve = sem("scaled_dve")
        scaled_act = sem("scaled_act")
        stored = sem("stored")

        block = ctx.enter_context(nc.Block())

        def cast(ap):
            return ap.bitcast(F32)

        def gain(v0, j):
            return vec[:, bass.ds(v0 + j * JT, JT)].unsqueeze(2).to_broadcast([P, JT, T])

        def rows(r, n):
            return r.unsqueeze(1).to_broadcast([P, JT, n])

        def tiles(buf, j, lo=0, n=T):
            return buf[:, bass.ds(j * JT, JT), lo:lo + n]

        def narrow(half):
            return ps[:, 4 * half:4 * half + 2, :].rearrange("p b (t n) -> p (b t) n", t=2)

        def paired(half, part):
            return ps[:, 4 * half:4 * half + 4, part * T:(part + 1) * T]

        def wide(half, lo):
            return ps[:, 4 * half:4 * half + 4, lo:TW]

        def x_bank(j):
            return ps[:, 2 + 4 * (j % 2):4 + 4 * (j % 2), :].rearrange("p b (t n) -> p (b t) n", t=2)

        def run(eng, counts, body):
            for st in stages:
                if st.iters == 1:
                    body(st, 0)
                else:
                    with eng.Fori(0, st.iters) as i:
                        counts.enter(st, i)
                        body(st, i)
                    counts.leave(st)

        @block.sync
        def _(sp):
            cnt = Counts()

            def load_x(j):
                cols = slice(j * PW, (j + 1) * PW)
                sp.dma_start(x_tok[:, :, cols], x[0, :, cols].rearrange("(m p) n -> p m n", p=P)
                             ).then_inc(x_landed[j], 16)

            def load_vectors():
                for v, r0 in ((norm_mix[0], V_MIX), (norm_mlp[0], V_MLP), (final_norm, V_FIN1), (norm_mix_2, V_MIX2), (norm_ffn_2, V_FFN2),
                              (norm_final_2, V_FIN2)):
                    sp.dma_start(gv[r0:r0 + NT, 0, :], v.rearrange("(t p) -> t p", p=P)).then_inc(vec_landed, 16)
                sp.dma_start(gv[0:NT, 1, :], pool_scale.rearrange("(t p) -> t p", p=P)).then_inc(vec_landed, 16)
                sp.dma_start(gv[NT:3 * NT, 1, :], b_gate.rearrange("(t p) -> t p", p=P)).then_inc(vec_landed, 16)
                sp.dma_start(gv[3 * NT:6 * NT, 1, :], conv_w.rearrange("k (t p) -> (k t) p", p=P)
                             ).then_inc(vec_landed, 16)
                sp.dma_start(meta_tok[:], meta).then_inc(meta_landed, 16)

            load_x(0)

            def body(st, i):
                for k, c in st.order:
                    p = st.panels[k]
                    src = dram[p.weight]
                    n = cnt.n["chunk"]
                    if 1 <= n < CH:
                        load_x(n)
                    if n == RAW:
                        load_vectors()
                    if st.iters > 1 or n >= RAW:
                        sp.wait_ge(w_lo, cnt.at("chunk", 1 - RAW) * UNITS)
                    r = p.row0 + c * KT * P
                    sp.dma_start(raw[:, n % RAW],
                                 src[r:r + KT * P, bass.ds(p.col(i), PW)].rearrange("(t p) n -> p t n", p=P)
                                 ).then_inc(raw_landed[n % RAW], 16)
                    cnt.n["chunk"] += 1

            def loops():
                for st in stages:
                    if st.iters == 1:
                        body(st, 0)
                    else:
                        with sp.Fori(0, st.iters) as i:
                            cnt.i = i
                            start = cnt.n["chunk"]
                            cnt.per = {"chunk": sum(p.chunks for p in st.panels)}
                            body(st, i)
                        cnt.i = None
                        cnt.n["chunk"] = start + st.iters * cnt.per["chunk"]

            loops()
            for half in range(2):
                for m, scaled in ((0, scaled_dve), (1, scaled_act)):
                    cols = slice(half * (D // 2), (half + 1) * (D // 2))
                    sp.wait_ge(scaled, half + 1)
                    sp.dma_start(out[0, m * P:(m + 1) * P, cols], o_tok[:, m, cols]).then_inc(stored, 16)
            sp.wait_ge(stored, 64)

        def unit_of(n, u):
            return (n * UNITS + u) % SPLIT

        def landed_count(cnt, ahead):
            n = cnt.n["chunk"] + ahead
            base = 16 * (n // RAW + 1)
            if cnt.i is None:
                return base
            assert cnt.per["chunk"] % RAW == 0
            return cnt.i * (16 * cnt.per["chunk"] // RAW) + base

        @block.scalar
        def _(act):
            cnt = Counts()
            act.dma_start(gm[:], norm_mix[0].rearrange("(t p) -> t p", p=P)).then_inc(mix_landed, 16)

            def split_hi(ahead=AHEAD // UNITS):
                n = cnt.n["chunk"] + ahead
                if n >= n_chunks:
                    return
                act.wait_ge(raw_landed[n % RAW], landed_count(cnt, ahead))
                for u in range(UNITS):
                    if cnt.i is not None or n * UNITS + u >= SPLIT:
                        act.wait_ge(w_used, cnt.at("chunk", ahead) * UNITS + (u + 1 - SPLIT))
                    act.activation(whi[:, unit_of(n, u)], raw[:, n % RAW, u * UK:(u + 1) * UK, :],
                                   ACT.Copy).then_inc(w_hi, 1)

            def operand_hi(j):
                act.wait_ge(full_ready, cnt.at("full", 1))
                act.activation(tiles(a_hi, j, M), full[:], ACT.Copy).then_inc(act_done, 1)
                cnt.event("x")

            def tokens_out(j):
                act.activation(tiles(h, j), x_bank(j), ACT.Copy).then_inc(act_done, 1)

            def token_squares(m):
                act.activation(x_sq[:, m, :], x_tok[:, m, :], ACT.Square,
                               accum_out=stat[:, m:m + 1]).then_inc(ssq_ready, 1)

            def cross_out(kind, half):
                if kind in PAIRED:
                    act.wait_ge(w_used, cnt.at("chunk") * UNITS)
                    act.wait_ge(full_ready, cnt.at("full"))
                    act.wait_ge(pool_done, cnt.at("pool"))
                    act.activation(full[:], paired(half, 1), ACT.Copy).then_inc(act_done, 1)

            def evac(kind, j):
                dst = {"q": tiles(b_hi, j), "k": k_hi[:], "v": v_hi[:], "res": tiles(a_hi, j, M),
                       "res2": tiles(a_hi, j, M), "up": tiles(a_hi, j, M), "relu2": tiles(b_hi, j), "co": tiles(a_hi, j, M), "resb": tiles(b_hi, j),
                       "gb": tiles(b_hi, j), "attn": tiles(b_hi, j)}
                if kind == "fin":
                    act.wait_ge(y_t, j + 1)
                    act.activation(o_tok[:, :, j * PW:(j + 1) * PW], ps[:, 2:4, :], ACT.Copy).then_inc(act_done, 1)
                    return
                if not KINDS[kind].get("act") or kind == "add":
                    return
                act.wait_ge(full_ready, cnt.at("full", 1))
                if kind == "ga":
                    act.activation(tiles(za, j), full[:], ACT.Sigmoid).then_inc(act_done, 1)
                elif kind == "gbr":
                    act.activation(tiles(G, j), full[:], ACT.Sigmoid).then_inc(act_done, 1)
                elif kind == "gate":
                    act.activation(S1[:, :, 0:T], U[:, :, 0:T], ACT.Sigmoid).then_inc(act_done, 1)
                else:
                    src = full[:].rearrange("p a b -> p (a b)").rearrange("p (a b) -> p a b", b=PW) if kind == "v" else full[:]
                    act.activation(dst[kind], src, ACT.Copy).then_inc(act_done, 1)
                if kind in ("res", "resb", "res2"):
                    act.wait_ge(sq_step, cnt.at("sq"))
                    act.activation(sqt, tiles(h, j), ACT.Square).then_inc(act_done, 1)

            def root(k):
                act.wait_ge(ms_ready, NORM_AT[k])
                act.activation(ms[:, 1, M:TW], ms[:, 0, M:TW], ACT.Sqrt).then_inc(root_ready, 1)
                if k == 1:
                    act.wait_ge(ms_ready, NORM_AT[k] + 1)
                    act.activation(ms[:, 1, :], ms[:, 0, :], ACT.Sqrt).then_inc(root_ready, 1)

            def weights_exp(g):
                act.wait_ge(arg_ready, g + 1)
                for b, hd in ((2, 0), (6, 2)):
                    last = act.activation(t1[:, hd:hd + 2, :], ps[:, b:b + 2, 0:3 * P], ACT.Exp)
                last.then_inc(a_exp, 1)

            def weights_hi(g):
                act.wait_ge(a_full, g + 1)
                act.activation(p_hi[:], t1[:], ACT.Copy).then_inc(aw_hi, 1)

            def softplus_ln(g):
                act.wait_ge(z_read, g + 1)
                act.activation(t1[:], t1[:], ACT.Exp).then_inc(act_chain, 1)
                act.wait_ge(act_chain, g + 1)
                act.activation(t1[:], t1[:], ACT.Ln, bias=1.0).then_inc(sp_ln, 1)

            def softplus_hi(g):
                act.wait_ge(sp_full, g + 1)
                act.activation(p_hi[:], t2[:], ACT.Copy).then_inc(sp_hi, 1)

            operand_hi(0)
            split_hi(0)
            tokens_out(0)
            operand_hi(1)
            split_hi(1)
            tokens_out(1)
            split_early = [False]

            def body(st, i):
                for q, (k, c) in enumerate(st.order):
                    p = st.panels[k]
                    if not split_early[0]:
                        split_hi()
                    split_early[0] = False
                    cnt.n["chunk"] += 1
                    if st.name == "q" and k == 0:
                        if c < 2:
                            operand_hi(c + 2)
                            tokens_out(c + 2)
                        if c == 2:
                            for m in range(MT):
                                token_squares(m)
                            act.wait_ge(ms_ready, 1)
                            act.activation(stat[:, 4:6], stat[:, 2:4], ACT.Sqrt).then_inc(root_ready, 1)
                    if st.name == "q" and k == 1 and c == 2:
                        act.wait_ge(meta_step, 2)
                        act.activation(a_hi[:, :, 0:M], S1[:, 0, 0:NT * M].rearrange("p (t n) -> p t n", n=M),
                                       ACT.Copy).then_inc(meta_hi, 1)
                    if st.norm is not None and k == 0 and c == NORM_CHUNK:
                        root(st.norm)
                    if st.name == "dn_2" and k == 3 and c == 0:
                        act.activation(ms[:, 1, 0:2], ms[:, 0, 0:2], ACT.Sqrt)
                    for g, step in attn_steps(st, q):
                        if step == 7:
                            weights_hi(g)
                    if c == p.chunks - 1:
                        cross_out(p.kind, k % 2)
                        if p.kind == "fin":
                            act.wait_ge(dve_mid, cnt.at("mid", 1))
                            act.activation(sqt, tiles(h, k), ACT.Square).then_inc(act_done, 1)
                        if attn_over(st, q):
                            split_hi()
                            split_early[0] = True
                        evac(p.kind, k // 2 if p.kind in ("k", "v") else st.index(i, k))
                        cnt.event(p.kind)
                    for g, step in attn_steps(st, q):
                        if step == 2:
                            softplus_ln(g)
                        if step == 4:
                            softplus_hi(g)
                        if step == 6:
                            weights_exp(g)
                        if step == 8:
                            evac("attn", g)
                            cnt.event("attn")

            run(act, cnt, body)
            act.wait_ge(ms_ready, NORM_AT[3])
            act.activation(stat[:, 4:6], stat[:, 2:4], ACT.Sqrt).then_inc(root_ready, 1)
            act.wait_ge(col_ready, 1)
            act.wait_ge(act_done, cnt.at("act"))
            for half in range(2):
                cols = slice(half * (D // 2), (half + 1) * (D // 2))
                act.activation(o_tok[:, 1, cols], o_tok[:, 1, cols], ACT.Copy,
                               scale=stat[:, 1:2]).then_inc(scaled_act, 1)

        @block.vector
        def _(dve):
            cnt = Counts()
            mid = [0]

            def step(ins):
                mid[0] += 1
                ins.then_inc(dve_mid, 1)
                dve.wait_ge(dve_mid, cnt.at("mid", mid[0]))

            def split_lo(ahead=AHEAD // UNITS):
                n = cnt.n["chunk"] + ahead
                if n >= n_chunks:
                    return
                dve.wait_ge(raw_landed[n % RAW], landed_count(cnt, ahead))
                for u in range(UNITS):
                    dve.wait_ge(w_hi, cnt.at("chunk", ahead) * UNITS + (u + 1))
                    s = unit_of(n, u)
                    dve.tensor_tensor(wlo[:, s], raw[:, n % RAW, u * UK:(u + 1) * UK, :], cast(whi[:, s]),
                                      ALU.subtract).then_inc(w_lo, 1)

            dve.memset(ones[:], 1.0)
            dve.memset(acc[:], 0.0).then_inc(consts, 1)
            dve.wait_ge(vec_t, 1)
            dve.tensor_copy(vec[:, 0:NT], ps[:, 5, 0:NT]).then_inc(vec_ready, 1)
            dve.wait_ge(vec_ready, 1)

            def operand(j):
                dve.wait_ge(tr_done, j + 1)
                if j > 0:
                    dve.wait_ge(pool_done, cnt.at("pool"))
                dve.tensor_tensor(full[:], x_bank(j), gain(V_MIX, j), ALU.mult).then_inc(full_ready, 1)
                cnt.event("x")

            operand(0)
            split_lo(0)
            operand(1)
            split_lo(1)

            def vectors():
                dve.wait_ge(vec_t, 2)
                dve.tensor_copy(vec[:], ps[:, 7, T:T + 192]).then_inc(vec_ready, 1)
                dve.wait_ge(vec_ready, 2)

            def token_rms():
                dve.wait_ge(ssq_ready, 2)
                dve.tensor_scalar(stat[:, 2:4], stat[:, 0:2], 1.0 / D, EPS, ALU.mult, ALU.add).then_inc(ms_ready, 1)
                dve.wait_ge(root_ready, 1)
                dve.reciprocal(stat[:, 6:8], stat[:, 4:6]).then_inc(rstd_ready, 1)
                dve.wait_ge(rstd_ready, 1)
                for m in range(MT):
                    last = dve.tensor_scalar(S2[:, m, 0:P], ident[:], stat[:, 6 + m:7 + m], None, ALU.mult)
                last.then_inc(diag_ready, 1)

            def token_rows():
                dve.wait_ge(rr_mm, 1)
                dve.tensor_copy(rr[:, M:TW], ps[:, 7, 0:T]).then_inc(diag_ready, 1)
                dve.wait_ge(diag_ready, 2)

            def meta_operand():
                meta_raw = U[:, 0, 0:NT * M]
                meta_f = S1[:, 0, 0:NT * M].rearrange("p (t n) -> p t n", n=M)
                dve.wait_ge(meta_t, 1)
                dve.tensor_copy(meta_raw, ps[:, 6, T:T + NT * M]).then_inc(meta_step, 1)
                dve.wait_ge(meta_step, 1)
                dve.tensor_tensor(meta_f, meta_raw.rearrange("p (t n) -> p t n", n=M),
                                  vec[:, V_MIX2:V_MIX2 + NT].unsqueeze(2).to_broadcast([P, NT, M]),
                                  ALU.mult).then_inc(meta_step, 1)
                dve.wait_ge(meta_step, 2)
                dve.tensor_tensor(U[:, 1, 0:NT * M], meta_raw, meta_raw, ALU.mult).then_inc(meta_step, 1)
                dve.wait_ge(meta_hi, 1)
                dve.tensor_tensor(a_lo[:, :, 0:M], meta_f, cast(a_hi[:, :, 0:M]), ALU.subtract).then_inc(meta_step, 1)
                dve.wait_ge(meta_step, 4)
                dve.tensor_reduce(msum[:], U[:, 1, 0:NT * M].rearrange("p (t n) -> p n t", n=M), mybir.AxisListType.X,
                                  ALU.add).then_inc(meta_step, 1)

            def z_out(g):
                dve.wait_ge(z_ready, g + 1)
                dve.wait_ge(meta_step, 5)
                if g > 0:
                    dve.wait_ge(aw_lo, g)
                for b, hd in ((2, 0), (6, 2)):
                    last = dve.tensor_scalar(t2[:, hd:hd + 2, :], ps[:, b:b + 2, 0:3 * P], 0.0, None, ALU.max)
                last.then_inc(z_mid, 1)
                dve.wait_ge(z_mid, g + 1)
                for b, hd in ((2, 0), (6, 2)):
                    last = dve.scalar_tensor_tensor(out=t1[:, hd:hd + 2, :], in0=t2[:, hd:hd + 2, :], scalar=-2.0,
                                                    in1=ps[:, b:b + 2, 0:3 * P], op0=ALU.mult, op1=ALU.add)
                last.then_inc(z_read, 1)

            def softplus_sum(g):
                dve.wait_ge(sp_ln, g + 1)
                dve.tensor_tensor(t2[:], t2[:], t1[:], ALU.add).then_inc(sp_raw, 1)

            def softplus_lo(g):
                dve.wait_ge(sp_hi, g + 1)
                dve.tensor_tensor(p_lo[:], t2[:], cast(p_hi[:]), ALU.subtract).then_inc(sp_lo, 1)

            def weights_lo(g):
                dve.wait_ge(aw_hi, g + 1)
                dve.tensor_tensor(p_lo[:], t1[:], cast(p_hi[:]), ALU.subtract).then_inc(aw_lo, 1)

            def attn_out(g):
                mid[0] = 0
                dve.wait_ge(o_ready, g + 1)
                dve.wait_ge(pool_done, cnt.at("pool"))
                dve.tensor_copy(full[:, 0:2, :], ps[:, 2:4, 0:T]).then_inc(dve_mid, 1)
                dve.tensor_copy(full[:, 2:4, :], ps[:, 6:8, 0:T]).then_inc(full_ready, 1)
                cnt.event("attn")

            def norm(k):
                dve.wait_ge(norm_mm, k + 1)
                dve.tensor_scalar(ms[:, 0, M:TW], ps[:, 7, 0:T], 1.0 / D, EPS, ALU.mult, ALU.add).then_inc(ms_ready, 1)
                dve.wait_ge(root_ready, NORM_AT[k])
                if k != 1:
                    dve.reciprocal(rr[:, M:TW], ms[:, 1, M:TW]).then_inc(rstd_ready, 1)
                else:
                    dve.reciprocal(rr1[:], ms[:, 1, M:TW]).then_inc(norm_mid, 1)
                    dve.wait_ge(norm_mid, 1)
                    dve.tensor_tensor(ms[:, 0, M:TW], ps[:, 6, M:TW], rr1[:], ALU.mult).then_inc(norm_mid, 1)
                    dve.wait_ge(norm_mid, 2)
                    dve.tensor_tensor(ms[:, 0, M:TW], ms[:, 0, M:TW], rr1[:], ALU.mult)
                    dve.tensor_copy(ms[:, 0, 0:M], ps[:, 6, 0:M]).then_inc(norm_mid, 1)
                    dve.wait_ge(norm_mid, 3)
                    dve.tensor_scalar(ms[:, 0, :], ms[:, 0, :], 1.0 / D, EPS, ALU.mult, ALU.add).then_inc(ms_ready, 1)
                    dve.wait_ge(root_ready, NORM_AT[k] + 1)
                    dve.reciprocal(rr[:], ms[:, 1, :]).then_inc(norm_mid, 1)
                    dve.wait_ge(norm_mid, 4)
                    dve.tensor_tensor(rr[:, M:TW], rr[:, M:TW], rr1[:], ALU.mult).then_inc(rstd_ready, 1)
                dve.wait_ge(rstd_ready, k + 2)

            def evac(kind, half, j):
                mid[0] = 0
                dve.wait_ge(w_used, cnt.at("chunk") * UNITS)
                dve.wait_ge(full_ready, cnt.at("full"))
                dve.wait_ge(act_done, cnt.at("act", 1 if kind in PAIRED else 0))
                dve.wait_ge(pool_done, cnt.at("pool"))
                n = paired(half, 0) if kind in PAIRED else narrow(half)
                r = rows(rr[:, M:TW], T)
                if kind in PAIRED and kind not in ("add", "gate", "res2"):
                    step(dve.tensor_tensor(full[:], n, full[:], ALU.add))
                if kind == "q":
                    last = dve.scalar_tensor_tensor(out=full[:], in0=n, scalar=QK_SCALE, in1=r,
                                                    op0=ALU.mult, op1=ALU.mult)
                elif kind == "k":
                    last = dve.tensor_tensor(full[:], n, r, ALU.mult)
                elif kind == "v":
                    for m in range(MT):
                        last = dve.tensor_scalar(full[:].rearrange("p (m t) n -> p m (t n)", m=MT)[:, m, :],
                                                 ps[:, 4 * half + m, :], stat[:, 6 + m:7 + m], None, ALU.mult)
                elif kind == "add":
                    step(dve.tensor_tensor(tiles(h, j), tiles(h, j), n, ALU.add))
                    last = dve.tensor_tensor(tiles(h, j), tiles(h, j), full[:], ALU.add)
                elif kind in ("res", "resb"):
                    step(dve.tensor_tensor(tiles(h, j), tiles(h, j), n if kind == "res" else full[:], ALU.add))
                    last = dve.tensor_tensor(full[:], tiles(h, j), gain(V_MLP if kind == "res" else V_FFN2, j), ALU.mult)
                elif kind == "res2":
                    dve.wait_ge(sq_step, cnt.at("sq"))
                    step(dve.tensor_tensor(U[:, :, 0:T], full[:], n, ALU.add))
                    step(dve.tensor_tensor(U[:, :, 0:T], tiles(h, j), U[:, :, 0:T], ALU.add))
                    step(dve.tensor_tensor(tiles(h, j), U[:, :, 0:T], gain(V_FIN1, j), ALU.mult))
                    last = dve.tensor_tensor(full[:], tiles(h, j), gain(V_MIX2, j), ALU.mult)
                elif kind == "relu2":
                    step(dve.tensor_tensor(full[:], full[:], r, ALU.mult))
                    last = dve.scalar_tensor_tensor(out=full[:], in0=full[:], scalar=0.0, in1=full[:],
                                                    op0=ALU.max, op1=ALU.mult)
                elif kind in ("u0", "u1", "u2", "u3"):
                    lo = WIDE[kind]
                    step(dve.tensor_tensor(U[:, :, lo:TW], wide(half, lo), rows(rr[:, lo:TW], TW - lo), ALU.mult))
                    src, bufs, w = U, [S1, S2], 1
                    while w < WINDOWS[j]:
                        lo += w
                        dst = bufs[0]
                        step(dve.tensor_tensor(dst[:, :, lo:TW], src[:, :, lo:TW], src[:, :, lo - w:TW - w], ALU.add))
                        src, bufs, w = dst, bufs[::-1], 2 * w
                    last = dve.scalar_tensor_tensor(out=full[:], in0=src[:, :, M:TW], scalar=1.0 / w,
                                                    in1=U[:, :, M:TW], op0=ALU.mult, op1=ALU.subtract)
                elif kind in ("ga", "gbr"):
                    step(dve.tensor_tensor(full[:], full[:], r, ALU.mult))
                    last = dve.tensor_tensor(full[:], full[:], gain(V_BG if kind == "ga" else V_BG + NT, j), ALU.add)
                elif kind == "pw":
                    last = dve.tensor_tensor(tiles(za, j), tiles(za, j), n, ALU.mult)
                elif kind == "gc":
                    lo = WIDE[kind]
                    last = dve.tensor_tensor(tiles(G, j, lo, TW - lo), wide(half, lo), rows(rr[:, lo:TW], TW - lo),
                                             ALU.mult)
                elif kind == "vv":
                    lo = WIDE[kind]
                    step(dve.tensor_tensor(U[:, :, lo:TW], wide(half, lo), rows(rr[:, lo:TW], TW - lo), ALU.mult))
                    last = dve.tensor_tensor(U[:, :, lo:TW], U[:, :, lo:TW], tiles(G, j, lo, TW - lo), ALU.mult)
                elif kind == "gb":
                    step(dve.tensor_tensor(full[:], full[:], r, ALU.mult))
                    last = dve.tensor_tensor(full[:], full[:], tiles(G, j), ALU.mult)
                elif kind == "co":
                    step(dve.tensor_tensor(full[:], full[:], tiles(G, j), ALU.mult))
                    last = dve.tensor_tensor(full[:], full[:], tiles(za, j), ALU.add)
                elif kind == "gate":
                    step(dve.tensor_tensor(U[:, :, 0:T], n, full[:], ALU.add))
                    last = dve.tensor_tensor(U[:, :, 0:T], U[:, :, 0:T], r, ALU.mult)
                elif kind == "up":
                    step(dve.tensor_tensor(full[:], full[:], r, ALU.mult))
                    last = dve.tensor_tensor(full[:], full[:], S1[:, :, 0:T], ALU.mult)
                elif kind == "fin":
                    step(dve.tensor_tensor(tiles(h, j), tiles(h, j), n, ALU.add))
                    if j > 0:
                        dve.wait_ge(y_t, j)
                    last = dve.tensor_tensor(full[:], tiles(h, j), gain(V_FIN2, j), ALU.mult)
                last.then_inc(full_ready, 1)
                if kind == "fin":
                    dve.wait_ge(act_done, cnt.at("act", 1))
                    dve.wait_ge(tri_ready, 8)
                    step(dve.tensor_tensor(acc[:, 1:3, :], S2[:, 0:2, 0:T], S2[:, 2:4, 0:T], ALU.add))
                    step(dve.tensor_tensor(acc[:, 0, :], acc[:, 0, :], acc[:, 1, :], ALU.add))
                    step(dve.tensor_tensor(acc[:, 0, :], acc[:, 0, :], acc[:, 2, :], ALU.add))

            def body(st, i):
                for q, (k, c) in enumerate(st.order):
                    p = st.panels[k]
                    for g, s in attn_steps(st, q):
                        if s == 5:
                            softplus_lo(g)
                    split_lo()
                    cnt.n["chunk"] += 1
                    if st.name == "q" and k == 0:
                        if c < 2:
                            operand(c + 2)
                        if c == 2:
                            token_rms()
                        if c == 3:
                            token_rows()
                    if st.name == "q" and k == 1 and c == 2:
                        vectors()
                        meta_operand()
                    if st.norm is not None and k == 0 and c == NORM_CHUNK:
                        norm(st.norm)
                    if c == p.chunks - 1:
                        evac(p.kind, k % 2, k // 2 if p.kind in ("k", "v") else st.index(i, k))
                        cnt.event(p.kind)
                    for g, s in attn_steps(st, q):
                        if s == 1:
                            z_out(g)
                        if s == 3:
                            softplus_sum(g)
                        if s == 7:
                            weights_lo(g)
                        if s == 8:
                            attn_out(g)

            run(dve, cnt, body)
            dve.wait_ge(y_sums, 1)
            dve.tensor_scalar(stat[:, 2:4], ps[:, 7, 0:4].rearrange("p (m n) -> p m n", n=2)[:, :, 0], 1.0 / D, EPS,
                              ALU.mult, ALU.add).then_inc(ms_ready, 1)
            dve.wait_ge(root_ready, NORM_AT[3])
            dve.reciprocal(stat[:, 0:2], stat[:, 4:6]).then_inc(col_ready, 1)
            dve.wait_ge(col_ready, 1)
            dve.wait_ge(act_done, cnt.at("act"))
            for half in range(2):
                cols = slice(half * (D // 2), (half + 1) * (D // 2))
                dve.tensor_scalar(o_tok[:, 0, cols], o_tok[:, 0, cols], stat[:, 0:1], None,
                                  ALU.mult).then_inc(scaled_dve, 1)

        @block.gpsimd
        def _(pool):
            cnt = Counts()
            pool.memset(ident[:], 0.0).then_inc(tri_ready, 1)
            pool.wait_ge(tri_ready, 1)
            pool.affine_select(out=ident[:], in_=ident[:], compare_op=ALU.not_equal, fill=1.0, base=0,
                               pattern=[[-1, P]], channel_multiplier=1).then_inc(consts, 1)
            pool.memset(tri32[:], -1.0).then_inc(tri_ready, 1)
            pool.wait_ge(tri_ready, 2)
            pool.tensor_copy(negone[:], tri32[:]).then_inc(tri_ready, 1)
            pool.wait_ge(tri_ready, 3)
            pool.affine_select(out=tri32[:], in_=tri32[:], compare_op=ALU.is_ge, fill=0.0, base=0,
                               pattern=[[-1, P]], channel_multiplier=1).then_inc(tri_ready, 1)
            pool.wait_ge(tri_ready, 4)
            pool.tensor_copy(negtri[:], tri32[:]).then_inc(tri_ready, 1)
            for j in range(CH):
                pool.wait_ge(act_done, cnt.at("act", 1))
                pool.tensor_tensor(tiles(a_lo, j, M), full[:], cast(tiles(a_hi, j, M)),
                                   ALU.subtract).then_inc(pool_done, 1)
                cnt.event("x")

            def lo_part(kind, j):
                to_b = ("q", "relu2", "gb", "attn", "resb", "u0", "u1", "u2", "u3")
                if kind == "k":
                    lo, hi, src = k_lo[:], k_hi[:], full[:]
                elif kind == "v":
                    lo, hi = v_lo[:], v_hi[:]
                    src = full[:].rearrange("p a b -> p (a b)").rearrange("p (a b) -> p a b", b=PW)
                elif kind in to_b:
                    lo, hi, src = tiles(b_lo, j), tiles(b_hi, j), full[:]
                else:
                    lo, hi, src = tiles(a_lo, j, M), tiles(a_hi, j, M), full[:]
                if kind in ("u0", "u1", "u2", "u3"):
                    pool.wait_ge(full_ready, cnt.at("full", 1))
                    pool.tensor_copy(hi, src).then_inc(pool_done, 1)
                    pool.wait_ge(pool_done, cnt.at("pool", 1))
                else:
                    pool.wait_ge(act_done, cnt.at("act", 2 if kind in PAIRED else 1))
                pool.tensor_tensor(lo, src, cast(hi), ALU.subtract).then_inc(pool_done, 1)

            def add_squares(dst, sq, n):
                pool.wait_ge(act_done, cnt.at("act", n))
                pool.tensor_tensor(dst, dst, sq, ALU.add).then_inc(sq_step, 1)

            def conv(j):
                y, t = S1[:, :, 0:T], S2[:, :, 0:T]
                pool.wait_ge(full_ready, cnt.at("full", 1))
                for tap in range(3):
                    dst = y if tap == 0 else t
                    pool.tensor_tensor(dst, U[:, :, M - 2 + tap:TW - 2 + tap], gain(V_CV + tap * NT, j),
                                       ALU.mult).then_inc(pool_done, 1)
                    pool.wait_ge(pool_done, cnt.at("pool", 2 * tap if tap else 1))
                    if tap > 0:
                        pool.tensor_tensor(tiles(G, j) if tap == 2 else y, y, t, ALU.add).then_inc(pool_done, 1)
                        pool.wait_ge(pool_done, cnt.at("pool", 2 * tap + 1))

            def mask(t, before, after, g):
                pool.wait_ge(before, g + 1)
                for hd in range(GH):
                    v = t[:, hd, :].rearrange("p (b n) -> p b n", n=P)[:, 0:3:2, :]
                    last = pool.affine_select(out=v, in_=v, compare_op=ALU.is_gt, fill=0.0, base=0,
                                              pattern=[[0, 2], [1, P]], channel_multiplier=-1)
                last.then_inc(after, 1)

            def evac(kind, j):
                if kind == "ga":
                    pool.wait_ge(rstd_ready, 3)
                    pool.tensor_tensor(tiles(h, j), tiles(h, j), rows(rr1[:], T), ALU.mult).then_inc(pool_done, 1)
                    pool.wait_ge(act_done, cnt.at("act", 2))
                    pool.tensor_tensor(tiles(za, j), tiles(za, j), gain(V_PS, j), ALU.mult).then_inc(pool_done, 1)
                elif kind == "gate":
                    pool.wait_ge(act_done, cnt.at("act", 2))
                    pool.tensor_tensor(S1[:, :, 0:T], S1[:, :, 0:T], U[:, :, 0:T], ALU.mult).then_inc(pool_done, 1)
                elif kind == "vv":
                    conv(j)
                elif KINDS[kind].get("pool"):
                    if kind == "res2":
                        pool.wait_ge(full_ready, cnt.at("full", 1))
                        pool.tensor_tensor(U[:, :, 0:T], U[:, :, 0:T], U[:, :, 0:T], ALU.mult).then_inc(sq_step, 1)
                    else:
                        lo_part(kind, j)
                if kind in ("res", "resb"):
                    add_squares(acc[:], sqt, 2 if kind == "res" else 3)
                if kind == "res2":
                    pool.wait_ge(sq_step, cnt.at("sq", 1))
                    pool.tensor_tensor(acc[:], acc[:], U[:, :, 0:T], ALU.add).then_inc(sq_step, 1)
                    add_squares(acc2, sqt, 3)
                    lo_part(kind, j)

            def body(st, i):
                for q, (k, c) in enumerate(st.order):
                    p = st.panels[k]
                    cnt.n["chunk"] += 1
                    if c == p.chunks - 1:
                        evac(p.kind, k // 2 if p.kind in ("k", "v") else st.index(i, k))
                        cnt.event(p.kind)
                    for g, s in attn_steps(st, q):
                        if s == 4:
                            mask(t2, sp_raw, sp_full, g)
                        if s == 6:
                            mask(t1, a_exp, a_full, g)
                        if s == 8:
                            lo_part("attn", g)
                            cnt.event("attn")

            def fresh_sums(norms):
                pool.wait_ge(norm_mm, norms)
                if norms == 1:
                    pool.memset(acc2, 0.0)
                pool.memset(acc[:], 0.0).then_inc(tri_ready, 1)
                pool.wait_ge(tri_ready, 5 + norms)

            pool.wait_ge(consts, 2)
            for st in stages:
                if st.name in ("w2_3", "wo2", "dn_2"):
                    fresh_sums({"w2_3": 1, "wo2": 2, "dn_2": 3}[st.name])
                if st.iters == 1:
                    body(st, 0)
                else:
                    with pool.Fori(0, st.iters) as i:
                        cnt.enter(st, i)
                        body(st, i)
                    cnt.leave(st)

        @block.tensor
        def _(pe):
            cnt = Counts()
            pe.wait_ge(consts, 2)
            def operand(j):
                pe.wait_ge(x_landed[j], 16)
                if j >= 2:
                    pe.wait_ge(act_done, KINDS["x"]["act"] * (j - 1))
                for t in range(JT):
                    for m in range(MT):
                        last = pe.transpose(x_bank(j)[:, t, m * P:(m + 1) * P],
                                            x_tok[:, m, (j * JT + t) * P:(j * JT + t + 1) * P], ident[:])
                last.then_inc(tr_done, 1)
                cnt.event("x")

            pe.wait_ge(mix_landed, 16)
            pe.transpose(ps[:, 5, 0:NT], gm[:], ident[0:NT, 0:NT]).then_inc(vec_t, 1)
            operand(0)
            operand(1)

            def vectors():
                pe.wait_ge(vec_landed, 16 * 9)
                pe.wait_ge(diag_ready, 2)
                for b in range(2):
                    last = pe.transpose(ps[:, 7, T + 96 * b:T + 96 * b + 96], gv[:, b, :], ident[0:96, 0:96])
                last.then_inc(vec_t, 1)

            def meta_turn():
                pe.wait_ge(meta_landed, 16)
                pe.wait_ge(act_done, KINDS["x"]["act"] * CH)
                for t in range(NT):
                    last = pe.transpose(ps[:, 6, T + t * M:T + (t + 1) * M], meta_tok[:, t * P:(t + 1) * P],
                                        ident[0:M, 0:M])
                last.then_inc(meta_t, 1)

            def token_rows():
                pe.wait_ge(diag_ready, 1)
                for m in range(MT):
                    last = pe.matmul(ps[:, 7, m * P:(m + 1) * P], ones[:], S2[:, m, 0:P], start=(m == 0),
                                     stop=(m == MT - 1), skip_group_check=True)
                last.then_inc(rr_mm, 1)

            bufs = {"A": (a_buf, M), "B": (b_buf, 0)}

            def three(out, w_h, w_l, x_h, x_l, start, stop):
                pe.matmul(out, w_h, x_h, start=start, stop=False, skip_group_check=True)
                pe.matmul(out, w_h, x_l, start=False, stop=False, skip_group_check=True)
                return pe.matmul(out, w_l, x_h, start=False, stop=stop, skip_group_check=True)

            def chunk(p, c, half):
                n = cnt.n["chunk"]
                if p.needs:
                    pe.wait_ge(pool_done, ready[p.needs][c if p.chunks > 1 else p.tile0 // JT])
                buf, off = bufs[p.src]
                hi, lo = buf[:, 0], buf[:, 1]
                for u in range(UNITS):
                    s = unit_of(n, u)
                    pe.wait_ge(w_lo, cnt.at("chunk") * UNITS + (u + 1))
                    for j in range(JT):
                        for kt in range(UK):
                            x = p.tile0 + c * KT + u * UK + kt
                            first = c == 0 and u == 0 and kt == 0
                            stop = c == p.chunks - 1 and u == UNITS - 1 and kt == UK - 1
                            if p.kind == "v":
                                if j >= MT:
                                    break
                                tok = slice(off + j * P, off + (j + 1) * P)
                                last = three(ps[:, 4 * half + j, :], hi[:, x, tok], lo[:, x, tok],
                                             whi[:, s, kt, :], wlo[:, s, kt, :], first, stop)
                                continue
                            cols = slice(j * P, (j + 1) * P)
                            if p.kind in PAIRED:
                                bank, tok = ps[:, 4 * half + j, :], slice(off, off + T)
                                pe.matmul(bank.rearrange("p (a n) -> p a n", a=2), whi[:, s, kt, cols],
                                          buf[:, :, x, tok], start=first, stop=False, skip_group_check=True)
                                last = pe.matmul(bank[:, T:2 * T], wlo[:, s, kt, cols], hi[:, x, tok],
                                                 start=False, stop=stop, skip_group_check=True)
                                continue
                            if p.kind in WIDE:
                                lo_col = WIDE[p.kind]
                                o, tok = ps[:, 4 * half + j, lo_col:TW], slice(lo_col, TW)
                            else:
                                o, tok = ps[:, 4 * half + j // 2, (j % 2) * T:(j % 2 + 1) * T], slice(off, off + T)
                                first = first and j % 2 == 0
                            last = three(o, whi[:, s, kt, cols], wlo[:, s, kt, cols], hi[:, x, tok], lo[:, x, tok],
                                         first, stop)
                    last.then_inc(w_used, 1)
                cnt.n["chunk"] += 1

            hb = (2, 3, 6, 7)

            def scores(g):
                pe.wait_ge(pool_done, cnt.at("pool", -1 if g > 0 else 0))
                if g > 0:
                    pe.wait_ge(full_ready, cnt.at("full"))
                for hd in range(GH):
                    t = g * GH + hd
                    three(ps[:, hb[hd], 0:T], k_hi[:, hd, 0:P], k_lo[:, hd, 0:P], b_hi[:, t, :], b_lo[:, t, :],
                          True, False)
                    last = three(ps[:, hb[hd], T:T + P], k_hi[:, hd, P:T], k_lo[:, hd, P:T],
                                 b_hi[:, t, P:T], b_lo[:, t, P:T], False, False)
                last.then_inc(z_ready, 1)

            def suffix_sums(g):
                pe.wait_ge(sp_lo, g + 1)
                pe.wait_ge(tri_ready, 5)
                for hd in range(GH):
                    for part in (p_hi, p_lo):
                        pe.matmul(ps[:, hb[hd], 0:T], negtri[:], part[:, hd, 0:T], start=False, stop=False,
                                  skip_group_check=True)
                        pe.matmul(ps[:, hb[hd], P:T], negone[:], part[:, hd, T:T + P], start=False, stop=False,
                                  skip_group_check=True)
                        last = pe.matmul(ps[:, hb[hd], T:T + P], negtri[:], part[:, hd, T:T + P], start=False,
                                         stop=part is p_lo, skip_group_check=True)
                last.then_inc(arg_ready, 1)

            def values(g):
                pe.wait_ge(aw_lo, g + 1)
                for hd in range(GH):
                    col = slice(hd * HD, (hd + 1) * HD)
                    three(ps[:, hb[hd], 0:T], v_hi[:, 0, col], v_lo[:, 0, col], p_hi[:, hd, 0:T], p_lo[:, hd, 0:T],
                          True, False)
                    last = three(ps[:, hb[hd], P:T], v_hi[:, 1, col], v_lo[:, 1, col], p_hi[:, hd, T:T + P],
                                 p_lo[:, hd, T:T + P], False, True)
                last.then_inc(o_ready, 1)

            def norm(k):
                pe.wait_ge(sq_step, cnt.n["sq"])
                for s in range(JT):
                    last = pe.matmul(ps[:, 7, 0:T], ones[:], acc[:, s, :], start=(s == 0), stop=(s == JT - 1),
                                     skip_group_check=True)
                if k == 1:
                    pe.wait_ge(meta_step, 5)
                    pe.matmul(ps[:, 6, 0:M], ones[:], msum[:], start=True, stop=True, skip_group_check=True)
                    for s in range(JT):
                        last = pe.matmul(ps[:, 6, M:TW], ones[:], acc2[:, s, :], start=False, stop=(s == JT - 1),
                                         skip_group_check=True)
                last.then_inc(norm_mm, 1)

            def turn(j):
                pe.wait_ge(full_ready, cnt.at("full"))
                pe.wait_ge(act_done, cnt.at("act", -2))
                for m in range(MT):
                    for t in range(JT):
                        last = pe.transpose(ps[:, 2 + m, t * P:(t + 1) * P], full[:, t, m * P:(m + 1) * P], ident[:])
                last.then_inc(y_t, 1)

            def token_sums():
                pe.wait_ge(dve_mid, cnt.at("mid"))
                for m in range(MT):
                    last = pe.matmul(ps[:, 7, 2 * m:2 * m + 2], acc[:, 0, m * P:(m + 1) * P], ones[:, 0:2],
                                     start=(m == 0), stop=True, skip_group_check=True)
                last.then_inc(y_sums, 1)

            def banks_free(st, k):
                back = -1
                if st.name == "q" and k < 2:
                    return
                if st.name == "kv" and k >= 2 and k % 2 == 0 or st.name == "w_o" and k == 0:
                    back = -2
                if st.name == "w_o" and k == 1:
                    back = 0
                if st.name == "pw" and k == 1:
                    pe.wait_ge(dve_mid, cnt.at("mid", 1 - KINDS["ga"]["mid"]))
                    return
                pe.wait_ge(full_ready, cnt.at("full", back))

            def body(st, i):
                for q, (k, c) in enumerate(st.order):
                    p = st.panels[k]
                    if c == 0:
                        banks_free(st, k)
                        if st.name == "q" and k == 1:
                            pe.wait_ge(vec_ready, 1)
                        if st.name == "u" and k == 0:
                            pe.wait_ge(meta_step, 5)
                        if st.norm == 1 and k == 1:
                            pe.wait_ge(norm_mid, 3)
                        elif st.norm is not None and k == 1:
                            pe.wait_ge(ms_ready, NORM_AT[st.norm])
                    chunk(p, c, k % 2)
                    if st.name == "q" and k == 0:
                        if c < 2:
                            operand(c + 2)
                        if c == 3:
                            token_rows()
                    if st.name == "q" and k == 1 and c == 1:
                        vectors()
                        meta_turn()
                    if c == 0 and st.name == "dn_2" and k > 0:
                        turn(k - 1)
                    if st.norm is not None and k == 0 and c == NORM_CHUNK:
                        norm(st.norm)
                    if c == p.chunks - 1:
                        cnt.event(p.kind)
                    for g, s in attn_steps(st, q):
                        if s == 1:
                            scores(g)
                        if s == 6:
                            suffix_sums(g)
                        if s == 8:
                            values(g)
                            cnt.event("attn")

            run(pe, cnt, body)
            turn(3)
            token_sums()


_INS = ["x", "meta_tokens_2", "norm_mix", "norm_mlp", "final_norm", "sb_w_qkv", "sb_w_o", "mlp_w1", "mlp_w2",
        "norm_mix_g_2", "w_in_2", "b_gate_2", "pool_w_2", "pool_scale_2", "conv_w_2", "conv_out_w_2", "w_o_2",
        "norm_ffn_g_2", "w_gate_up_2", "w_down_2", "norm_final_g_2"]


def kernel(**inputs):
    import numpy as np
    import concourse.bacc as bacc
    from concourse.bass_utils import run_bass_kernel_spmd

    nc = bacc.Bacc("TRN2", target_bir_lowering=False, num_devices=1)
    arrays, args = {}, []
    for name in _INS:
        a = np.ascontiguousarray(inputs[name])
        arrays[f"in_{name}_dram"] = a
        args.append(nc.dram_tensor(f"in_{name}_dram", a.shape, mybir.dt.from_np(a.dtype), kind="ExternalInput").ap())
    out = nc.dram_tensor("out_dram", (1, T, D), F32, kind="ExternalOutput").ap()
    build(nc, *args, out)
    r = run_bass_kernel_spmd(nc, [arrays], core_ids=[0])
    return r.results[0]["out_dram"]
```
